# Optimizing a Trainium2 kernel written in Bass

```python
import math
import jax, jax.numpy as jnp
from jax import lax
import numpy as np

D_MODEL = 1024
BATCH = 1
SEQ = 2048
DEPTH = 1

MIX_WIDTH = D_MODEL
ATTN_WIDTH = MIX_WIDTH // 2
SSM_WIDTH = MIX_WIDTH - ATTN_WIDTH
ATTN_HEADS = 4
ATTN_VDIM = ATTN_WIDTH // ATTN_HEADS
ATTN_QKDIM = ATTN_VDIM // 2
Q_BLOCK = 128
SSM_GROUP = 16
SSM_GROUPS = SSM_WIDTH // SSM_GROUP
SSM_STATE = 64
D_FF = 4 * D_MODEL
EPS = 1e-6
IN_WIDTH = 3 * ATTN_WIDTH + SSM_WIDTH

kernel_name = 'hybrid_diffattn_s5_encoder_block'

def rmsnorm(x, g):
    xf = x.astype(jnp.float32)
    y = xf * lax.rsqrt(jnp.mean(xf * xf, axis=-1, keepdims=True) + EPS)
    return (y * g.astype(jnp.float32)).astype(x.dtype)

def alibi_slopes(n_heads):
    return jnp.asarray([2.0 ** (-8.0 * (h + 1) / n_heads) for h in range(n_heads)], dtype=jnp.float32)

def diff_attention(q, k, v, lam):
    b, s, h, _, d = q.shape
    nblk = s // Q_BLOCK
    scale = d ** -0.5
    slopes = alibi_slopes(h)
    kpos = jnp.arange(s, dtype=jnp.int32)
    qb = q.reshape(b, nblk, Q_BLOCK, h, 2, d).transpose(1, 0, 2, 3, 4, 5)

    def block(args):
        qi, i = args
        qpos = i * Q_BLOCK + jnp.arange(Q_BLOCK, dtype=jnp.int32)
        dist = jnp.abs(qpos[:, None] - kpos[None, :]).astype(jnp.float32)
        bias = -slopes[:, None, None] * dist[None]
        sc = jnp.einsum('bqhcd,bkhcd->bhcqk', qi, k).astype(jnp.float32) * scale
        p = jax.nn.softmax(sc + bias[None, :, None], axis=-1)
        a = p[:, :, 0] - lam * p[:, :, 1]
        return jnp.einsum('bhqk,bkhe->bqhe', a.astype(v.dtype), v)

    o = lax.map(block, (qb, jnp.arange(nblk, dtype=jnp.int32)))
    return o.transpose(1, 0, 2, 3, 4).reshape(b, s, h, v.shape[-1])

def s5_direction(u, lam_re, lam_im, log_dt, b_re, b_im, c_re, c_im):
    dt = jnp.exp(log_dt)[:, None]
    mag = jnp.exp(lam_re * dt)
    ang = lam_im * dt
    ar = mag * jnp.cos(ang)
    ai = mag * jnp.sin(ang)
    nr = ar - 1.0
    den = lam_re * lam_re + lam_im * lam_im
    cr = (nr * lam_re + ai * lam_im) / den
    ci = (ai * lam_re - nr * lam_im) / den
    bbr = cr[..., None] * b_re - ci[..., None] * b_im
    bbi = cr[..., None] * b_im + ci[..., None] * b_re
    bu_r = jnp.einsum('bsgh,gph->bsgp', u, bbr)
    bu_i = jnp.einsum('bsgh,gph->bsgp', u, bbi)
    a_r = jnp.broadcast_to(ar, bu_r.shape)
    a_i = jnp.broadcast_to(ai, bu_r.shape)

    def combine(e1, e2):
        a1r, a1i, b1r, b1i = e1
        a2r, a2i, b2r, b2i = e2
        return (a2r * a1r - a2i * a1i,
                a2r * a1i + a2i * a1r,
                a2r * b1r - a2i * b1i + b2r,
                a2r * b1i + a2i * b1r + b2i)

    _, _, xr, xi = lax.associative_scan(combine, (a_r, a_i, bu_r, bu_i), axis=1)
    return jnp.einsum('bsgp,ghp->bsgh', xr, c_re) - jnp.einsum('bsgp,ghp->bsgh', xi, c_im)

def bi_s5_glu(u, lam_re, lam_im, log_dt, b_re, b_im, c_re, c_im, d_skip, w_glu, b_glu):
    bsz, s, _ = u.shape
    uf = u.astype(jnp.float32).reshape(bsz, s, SSM_GROUPS, SSM_GROUP)
    f32 = lambda t: t.astype(jnp.float32)
    y_f = s5_direction(uf, f32(lam_re[0]), f32(lam_im[0]), f32(log_dt[0]), f32(b_re[0]), f32(b_im[0]), f32(c_re[0]), f32(c_im[0]))
    y_b = s5_direction(uf[:, ::-1], f32(lam_re[1]), f32(lam_im[1]), f32(log_dt[1]), f32(b_re[1]), f32(b_im[1]), f32(c_re[1]), f32(c_im[1]))[:, ::-1]
    y = (y_f + y_b).reshape(bsz, s, SSM_WIDTH) + f32(d_skip) * u.astype(jnp.float32)
    z = jax.nn.gelu(y, approximate=False)
    out = z * jax.nn.sigmoid(z @ f32(w_glu) + f32(b_glu))
    return out.astype(u.dtype)

def setup_inputs(seed: int = 0) -> dict:
    key = jax.random.key(seed)
    ks = jax.random.split(key, 24)
    f = jnp.float32
    nrm = lambda k, shape, std: jax.random.normal(k, shape, f) * std
    x = jax.random.normal(ks[0], (BATCH, SEQ, D_MODEL), f)
    norm1_g = 1.0 + nrm(ks[1], (DEPTH, D_MODEL), 0.02)
    w_in = nrm(ks[2], (DEPTH, D_MODEL, IN_WIDTH), D_MODEL ** -0.5)
    lam_q1 = nrm(ks[3], (DEPTH, ATTN_QKDIM), 0.1)
    lam_k1 = nrm(ks[4], (DEPTH, ATTN_QKDIM), 0.1)
    lam_q2 = nrm(ks[5], (DEPTH, ATTN_QKDIM), 0.1)
    lam_k2 = nrm(ks[6], (DEPTH, ATTN_QKDIM), 0.1)
    subln_g = 1.0 + nrm(ks[7], (DEPTH, ATTN_VDIM), 0.02)
    n_idx = jnp.arange(SSM_STATE, dtype=f)
    sshape = (DEPTH, 2, SSM_GROUPS, SSM_STATE)
    ssm_lam_re = -0.5 * jnp.exp(nrm(ks[8], sshape, 0.02))
    ssm_lam_im = math.pi * n_idx + nrm(ks[9], sshape, 0.02)
    ssm_log_dt = jax.random.uniform(ks[10], (DEPTH, 2, SSM_GROUPS), f, math.log(1e-3), math.log(1e-1))
    bshape = (DEPTH, 2, SSM_GROUPS, SSM_STATE, SSM_GROUP)
    cshape = (DEPTH, 2, SSM_GROUPS, SSM_GROUP, SSM_STATE)
    ssm_b_re = nrm(ks[11], bshape, (2.0 * SSM_GROUP) ** -0.5)
    ssm_b_im = nrm(ks[12], bshape, (2.0 * SSM_GROUP) ** -0.5)
    ssm_c_re = nrm(ks[13], cshape, (2.0 * SSM_STATE) ** -0.5)
    ssm_c_im = nrm(ks[14], cshape, (2.0 * SSM_STATE) ** -0.5)
    ssm_d = nrm(ks[15], (DEPTH, SSM_WIDTH), 1.0)
    w_glu = nrm(ks[16], (DEPTH, SSM_WIDTH, SSM_WIDTH), SSM_WIDTH ** -0.5)
    b_glu = nrm(ks[17], (DEPTH, SSM_WIDTH), 0.02)
    w_out = nrm(ks[18], (DEPTH, MIX_WIDTH, D_MODEL), MIX_WIDTH ** -0.5)
    norm2_g = 1.0 + nrm(ks[19], (DEPTH, D_MODEL), 0.02)
    w_mlp1 = nrm(ks[20], (DEPTH, D_MODEL, D_FF), D_MODEL ** -0.5)
    w_mlp2 = nrm(ks[21], (DEPTH, D_FF, D_MODEL), D_FF ** -0.5)
    final_g = 1.0 + nrm(ks[22], (D_MODEL,), 0.02)
    return {'x': x, 'norm1_g': norm1_g, 'w_in': w_in, 'lam_q1': lam_q1, 'lam_k1': lam_k1,
            'lam_q2': lam_q2, 'lam_k2': lam_k2, 'subln_g': subln_g,
            'ssm_lam_re': ssm_lam_re, 'ssm_lam_im': ssm_lam_im, 'ssm_log_dt': ssm_log_dt,
            'ssm_b_re': ssm_b_re, 'ssm_b_im': ssm_b_im, 'ssm_c_re': ssm_c_re, 'ssm_c_im': ssm_c_im,
            'ssm_d': ssm_d, 'w_glu': w_glu, 'b_glu': b_glu, 'w_out': w_out, 'norm2_g': norm2_g,
            'w_mlp1': w_mlp1, 'w_mlp2': w_mlp2, 'final_g': final_g}

def reference(x, norm1_g, w_in, lam_q1, lam_k1, lam_q2, lam_k2, subln_g,
              ssm_lam_re, ssm_lam_im, ssm_log_dt, ssm_b_re, ssm_b_im, ssm_c_re, ssm_c_im,
              ssm_d, w_glu, b_glu, w_out, norm2_g, w_mlp1, w_mlp2, final_g):
    bsz, s, _ = x.shape
    h = x
    for l in range(DEPTH):
        lambda_init = 0.8 - 0.6 * math.exp(-0.3 * l)
        hn = rmsnorm(h, norm1_g[l])
        proj = hn @ w_in[l]
        q = proj[..., :ATTN_WIDTH].reshape(bsz, s, ATTN_HEADS, 2, ATTN_QKDIM)
        k = proj[..., ATTN_WIDTH:2 * ATTN_WIDTH].reshape(bsz, s, ATTN_HEADS, 2, ATTN_QKDIM)
        v = proj[..., 2 * ATTN_WIDTH:3 * ATTN_WIDTH].reshape(bsz, s, ATTN_HEADS, ATTN_VDIM)
        u = proj[..., 3 * ATTN_WIDTH:]
        lam = (jnp.exp(jnp.sum(lam_q1[l].astype(jnp.float32) * lam_k1[l].astype(jnp.float32)))
               - jnp.exp(jnp.sum(lam_q2[l].astype(jnp.float32) * lam_k2[l].astype(jnp.float32)))
               + lambda_init)
        att = diff_attention(q, k, v, lam)
        att = rmsnorm(att, subln_g[l]) * (1.0 - lambda_init)
        ssm = bi_s5_glu(u, ssm_lam_re[l], ssm_lam_im[l], ssm_log_dt[l], ssm_b_re[l], ssm_b_im[l],
                        ssm_c_re[l], ssm_c_im[l], ssm_d[l], w_glu[l], b_glu[l])
        mix = jnp.concatenate([att.reshape(bsz, s, ATTN_WIDTH).astype(h.dtype), ssm.astype(h.dtype)], axis=-1)
        h = h + mix @ w_out[l]
        hn2 = rmsnorm(h, norm2_g[l])
        h = h + jnp.square(jax.nn.relu(hn2 @ w_mlp1[l])) @ w_mlp2[l]
    return rmsnorm(h, final_g)


_drawn_inputs = setup_inputs


def setup_inputs(seed=0):
    import zlib

    import numpy as np

    out = dict(_drawn_inputs(seed))
    spreads = {}
    factors = {'norm1_g': 2.725,
     'lam_q1': 3.867,
     'lam_k1': 2.806,
     'lam_q2': 200.0,
     'subln_g': 5.143,
     'ssm_lam_re': 200.0,
     'ssm_lam_im': 72.248,
     'ssm_log_dt': 75.168,
     'ssm_b_re': 145.808,
     'ssm_b_im': 146.184,
     'ssm_c_re': 141.24,
     'ssm_c_im': 145.92,
     'b_glu': 36.029,
     'norm2_g': 3.42,
     'final_g': 22.323}
    for name, (base, spread) in spreads.items():
        noise = np.random.default_rng([zlib.crc32(name.encode()), seed]).standard_normal(out[name].shape)
        drawn = base * np.exp(spread * noise) if base else spread * noise
        out[name] = __import__('jax').numpy.asarray(drawn.astype(out[name].dtype))
    for name, factor in factors.items():
        out[name] = (out[name] * factor).astype(out[name].dtype)
    return out
```

```python
import math
from contextlib import ExitStack

import numpy as np

import concourse.bass as bass
from concourse import mybir

F32 = mybir.dt.float32
F32R = mybir.dt.float32r
F16 = mybir.dt.float16
I32 = mybir.dt.int32
ALU = mybir.AluOpType
ACT = mybir.ActivationFunctionType
AX_X = mybir.AxisListType.X

P = 128
D = 1024
S = 2048
TB = 512
NTB = S // TB
KD = D // P
ATT = 512
H = 4
DH = 64
EPS = 1e-6
IN_W = 3 * ATT + ATT
NQK = 2 * ATT // P


class Memory:

    def __init__(self, nc, ctx, tag):
        self.nc, self.ctx, self.tag = nc, ctx, tag

    def sb(self, name, shape, dt=F32):
        return self.ctx.enter_context(self.nc.sbuf_tensor(f"{self.tag}_{name}", shape, dt))

    def ps(self, name, shape, dt=F32):
        return self.ctx.enter_context(self.nc.psum_tensor(f"{self.tag}_{name}", shape, dt))

    def sem(self, name):
        return self.ctx.enter_context(self.nc.semaphore(f"{self.tag}_{name}"))


def phase_project(nc, x_t, norm1_g, w_in, qk_s, v_s, u_s):
    BANKS = 6
    GROUPS = NQK + 2 * (TB // P)
    NPIECE = IN_W // P
    with ExitStack() as ctx:
        m = Memory(nc, ctx, "pj")
        w_raw = m.sb("w_raw", [P, 2, KD, P])
        w_hi = m.sb("w_hi", [P, KD, IN_W], F32R)
        w_lo = m.sb("w_lo", [P, KD, IN_W], F32R)
        x_raw = m.sb("x_raw", [P, KD, TB])
        x_hi = m.sb("x_hi", [P, KD, TB], F32R)
        x_lo = m.sb("x_lo", [P, KD, TB], F32R)
        square = m.sb("square", [P, TB])
        square_sum = m.sb("square_sum", [P, TB])
        rms_b = m.sb("rms_b", [P, TB])
        rinv_b = m.sb("rinv_b", [P, TB])
        rms_t = m.sb("rms_t", [P, TB // P])
        rinv_t = m.sb("rinv_t", [P, TB // P])
        gain = m.sb("gain", [P, KD])
        ones = m.sb("ones", [P, P])
        eps_c = m.sb("eps_c", [P, 1])
        qk_out = m.sb("qk_out", [P, 2, TB])
        vu_out = m.sb("vu_out", [P, 2, ATT])
        acc = m.ps("acc", [P, BANKS, TB])
        stat_b = m.ps("stat_b", [P, TB])
        stat_t = m.ps("stat_t", [P, TB])

        gain_loaded = m.sem("gain_loaded")
        consts_ready = m.sem("consts_ready")
        x_loaded = m.sem("x_loaded")
        w_loaded = [m.sem("w_loaded0"), m.sem("w_loaded1")]
        w_hi_ready = m.sem("w_hi_ready")
        w_lo_ready = m.sem("w_lo_ready")
        x_hi_ready = m.sem("x_hi_ready")
        x_lo_ready = m.sem("x_lo_ready")
        pool_step = m.sem("pool_step")
        squares_ready = m.sem("squares_ready")
        stats_done = m.sem("stats_done")
        rms_ready = m.sem("rms_ready")
        rinv_ready = m.sem("rinv_ready")
        group_done = m.sem("group_done")
        qk_evacuated = m.sem("qk_evacuated")
        vu_evacuated = m.sem("vu_evacuated")
        qk_stored = [m.sem("qk_stored0"), m.sem("qk_stored1")]
        vu_stored = [m.sem("vu_stored0"), m.sem("vu_stored1")]
        block = ctx.enter_context(nc.Block())
        w_pieces = w_in.rearrange("(k p) n -> p k n", p=P)
        x_tiles = x_t.rearrange("(k p) t -> p k t", p=P)

        def evacuated_before(eng, tb, g):
            prev, back = (g - BANKS, tb) if g >= BANKS else (
                max(x for x in range(GROUPS) if x % BANKS == g % BANKS), tb - 1)
            if isinstance(back, int) and back < 0:
                return
            if prev < NQK:
                eng.wait_ge(qk_evacuated, back * NQK + prev + 1)
            else:
                eng.wait_ge(vu_evacuated, back * (GROUPS - NQK) + prev - NQK + 1)

        @block.sync
        def _(sp):
            sp.dma_start(gain[:], norm1_g).then_inc(gain_loaded, 16)

            def load_w(i):
                if i >= 2:
                    sp.wait_ge(w_lo_ready, i - 1)
                sp.dma_start(w_raw[:, i % 2], w_pieces[:, :, i * P:(i + 1) * P]).then_inc(w_loaded[i % 2], 16)

            def stores(tb, gs):
                for g in gs:
                    if g < NQK:
                        sp.wait_ge(qk_evacuated, tb * NQK + g + 1)
                        sp.dma_start(qk_s[g, :, bass.ds(tb * TB, TB)], qk_out[:, g % 2]).then_inc(qk_stored[g % 2], 16)
                    else:
                        e = g - NQK
                        sp.wait_ge(vu_evacuated, tb * (GROUPS - NQK) + e + 1)
                        dst = v_s if e % 2 == 0 else u_s
                        sp.dma_start(dst[bass.ds(tb * TB + (e // 2) * P, P), :], vu_out[:, e % 2])\
                            .then_inc(vu_stored[e % 2], 16)

            def load_x(tb):
                if not isinstance(tb, int) or tb > 0:
                    sp.wait_ge(x_hi_ready, tb * KD)
                    sp.wait_ge(x_lo_ready, tb * KD)
                    sp.wait_ge(squares_ready, tb)
                sp.dma_start(x_raw[:], x_tiles[:, :, bass.ds(tb * TB, TB)]).then_inc(x_loaded, 16)

            load_x(0)
            for i in range(NPIECE):
                load_w(i)
            stores(0, range(GROUPS // 2))
            with sp.Fori(1, NTB) as tb:
                load_x(tb)
                stores(tb - 1, range(GROUPS // 2, GROUPS))
                stores(tb, range(GROUPS // 2))
            stores(NTB - 1, range(GROUPS // 2, GROUPS))
            for s in range(2):
                sp.wait_ge(qk_stored[s], 16 * NTB * NQK // 2)
                sp.wait_ge(vu_stored[s], 16 * NTB * (GROUPS - NQK) // 2)

        @block.gpsimd
        def _(pool):
            pool.memset(ones[:], 1.0).then_inc(consts_ready, 1)
            pool.memset(eps_c[:], EPS).then_inc(consts_ready, 1)

            with pool.Fori(0, NTB) as tb:
                pool.wait_ge(x_loaded, tb * 16 + 16)
                steps = 2 * KD - 2
                pool.tensor_tensor(square_sum[:], x_raw[:, 0], x_raw[:, 0], ALU.mult).then_inc(pool_step, 1)
                for k in range(1, KD):
                    pool.wait_ge(pool_step, tb * steps + 2 * k - 1)
                    pool.tensor_tensor(square[:], x_raw[:, k], x_raw[:, k], ALU.mult).then_inc(pool_step, 1)
                    pool.wait_ge(pool_step, tb * steps + 2 * k)
                    pool.tensor_tensor(square_sum[:], square_sum[:], square[:], ALU.add)\
                        .then_inc(pool_step if k < KD - 1 else squares_ready, 1)
                pool.wait_ge(stats_done, tb + 1)

        @block.scalar
        def _(act):
            def split_w(i):
                act.wait_ge(w_loaded[i % 2], 16 * (i // 2 + 1))
                act.activation(w_hi[:, :, i * P:(i + 1) * P], w_raw[:, i % 2], ACT.Copy).then_inc(w_hi_ready, 1)

            def split_x(tb):
                act.wait_ge(x_loaded, tb * 16 + 16)
                if not isinstance(tb, int) or tb > 0:
                    act.wait_ge(group_done, tb * GROUPS)
                for k in range(KD):
                    act.activation(x_hi[:, k], x_raw[:, k], ACT.Copy, scale=gain[:, k:k + 1]).then_inc(x_hi_ready, 1)

            def stats(tb):
                act.wait_ge(stats_done, tb + 1)
                if not isinstance(tb, int) or tb > 0:
                    act.wait_ge(rinv_ready, tb)
                act.activation(rms_b[:], stat_b[:], ACT.Sqrt, bias=eps_c[:], scale=1.0 / D)
                act.activation(rms_t[:], stat_t[:, 0:TB // P], ACT.Sqrt, bias=eps_c[:], scale=1.0 / D)\
                    .then_inc(rms_ready, 1)

            def evacuate_vu(tb, e):
                act.wait_ge(group_done, tb * GROUPS + NQK + e + 1)
                if e < 2:
                    if not isinstance(tb, int) or tb > 0:
                        act.wait_ge(vu_stored[e % 2], tb * 16 * ((GROUPS - NQK) // 2))
                else:
                    act.wait_ge(vu_stored[e % 2], tb * 16 * ((GROUPS - NQK) // 2) + 16 * (e // 2))
                act.activation(vu_out[:, e % 2], acc[:, (NQK + e) % BANKS], ACT.Copy,
                               scale=rinv_t[:, e // 2:e // 2 + 1]).then_inc(vu_evacuated, 1)

            act.wait_ge(gain_loaded, 16)
            act.wait_ge(consts_ready, 2)
            split_x(0)
            for i in range(NPIECE):
                split_w(i)
            stats(0)
            act.wait_ge(rinv_ready, 1)
            for e in range(GROUPS - NQK):
                evacuate_vu(0, e)
            with act.Fori(1, NTB) as tb:
                split_x(tb)
                stats(tb)
                act.wait_ge(rinv_ready, tb + 1)
                for e in range(GROUPS - NQK):
                    evacuate_vu(tb, e)

        @block.vector
        def _(dve):
            def split_w(i):
                dve.wait_ge(w_hi_ready, i + 1)
                dve.tensor_tensor(w_lo[:, :, i * P:(i + 1) * P], w_raw[:, i % 2],
                                  w_hi[:, :, i * P:(i + 1) * P].bitcast(F32), ALU.subtract).then_inc(w_lo_ready, 1)

            def split_x(tb):
                for k in range(KD):
                    dve.wait_ge(x_hi_ready, tb * KD + k + 1)
                    dve.scalar_tensor_tensor(x_lo[:, k], x_raw[:, k], gain[:, k:k + 1], x_hi[:, k].bitcast(F32),
                                             ALU.mult, ALU.subtract).then_inc(x_lo_ready, 1)

            def invert(tb):
                dve.wait_ge(rms_ready, tb + 1)
                if not isinstance(tb, int) or tb > 0:
                    dve.wait_ge(vu_evacuated, tb * (GROUPS - NQK))
                dve.reciprocal(rinv_b[:], rms_b[:])
                dve.reciprocal(rinv_t[:], rms_t[:]).then_inc(rinv_ready, 1)
                dve.wait_ge(rinv_ready, tb + 1)

            def evacuate_qk(tb, g):
                dve.wait_ge(group_done, tb * GROUPS + g + 1)
                if g < 2:
                    if not isinstance(tb, int) or tb > 0:
                        dve.wait_ge(qk_stored[g % 2], tb * 16 * (NQK // 2))
                else:
                    dve.wait_ge(qk_stored[g % 2], tb * 16 * (NQK // 2) + 16 * (g // 2))
                dve.tensor_tensor(qk_out[:, g % 2], acc[:, g % BANKS], rinv_b[:], ALU.mult).then_inc(qk_evacuated, 1)

            dve.wait_ge(gain_loaded, 16)
            split_x(0)
            for i in range(NPIECE):
                split_w(i)
            invert(0)
            for g in range(NQK):
                evacuate_qk(0, g)
            with dve.Fori(1, NTB) as tb:
                split_x(tb)
                invert(tb)
                for g in range(NQK):
                    evacuate_qk(tb, g)

        @block.tensor
        def _(pe):
            def stats(tb):
                pe.wait_ge(squares_ready, tb + 1)
                if not isinstance(tb, int) or tb > 0:
                    pe.wait_ge(rms_ready, tb)
                for c in range(TB // P):
                    pe.matmul(stat_t[:, c:c + 1], square_sum[:, c * P:(c + 1) * P], ones[:, 0:1], start=True, stop=True)
                pe.matmul(stat_b[:], ones[:], square_sum[:], start=True, stop=True).then_inc(stats_done, 1)

            def group(tb, g):
                evacuated_before(pe, tb, g)
                first = isinstance(tb, int)
                if g < NQK:
                    if first:
                        pe.wait_ge(w_lo_ready, g + 1)
                    for k in range(KD):
                        if g == 0:
                            pe.wait_ge(x_lo_ready, tb * KD + k + 1)
                        cols = slice(g * P, (g + 1) * P)
                        pe.matmul(acc[:, g % BANKS], w_hi[:, k, cols], x_hi[:, k], start=(k == 0), stop=False)
                        pe.matmul(acc[:, g % BANKS], w_hi[:, k, cols], x_lo[:, k], start=False, stop=False)
                        last = pe.matmul(acc[:, g % BANKS], w_lo[:, k, cols], x_hi[:, k], start=False, stop=(k == KD - 1))
                else:
                    e = g - NQK
                    cols = slice(2 * ATT + (e % 2) * ATT, 2 * ATT + (e % 2 + 1) * ATT)
                    if first and e < 2:
                        pe.wait_ge(w_lo_ready, cols.stop // P)
                    rows = slice((e // 2) * P, (e // 2 + 1) * P)
                    for k in range(KD):
                        pe.matmul(acc[:, g % BANKS], x_hi[:, k, rows], w_hi[:, k, cols], start=(k == 0), stop=False)
                        pe.matmul(acc[:, g % BANKS], x_hi[:, k, rows], w_lo[:, k, cols], start=False, stop=False)
                        last = pe.matmul(acc[:, g % BANKS], x_lo[:, k, rows], w_hi[:, k, cols], start=False, stop=(k == KD - 1))
                last.then_inc(group_done, 1)

            pe.wait_ge(consts_ready, 2)
            for g in range(GROUPS):
                if g == BANKS:
                    stats(0)
                group(0, g)
            with pe.Fori(1, NTB) as tb:
                stats(tb)
                for g in range(GROUPS):
                    group(tb, g)


def phase_attention(nc, lam_in, qk_s, v_s, att_s, total_s):
    NQ = S // P
    QB = TB // P
    NB = NQ // QB
    HALF = S // 2
    SCALE = DH ** -0.5
    CENTER = S - P
    STRIP = CENTER + S
    LAM_INIT = 0.8 - 0.6 * math.exp(0.0)
    STEP0 = int(2.0 ** (-8.0 / H) / SCALE)
    assert STEP0 == 2 and SCALE == 0.125
    with ExitStack() as ctx:
        m = Memory(nc, ctx, "at")
        k_raw = m.sb("k_raw", [P, 2, S])
        k_hi = m.sb("k_hi", [P, 2, S], F32R)
        k_lo = m.sb("k_lo", [P, 2, S], F32R)
        q_raw = m.sb("q_raw", [P, 4, 2, P])
        q_hl = m.sb("q_hl", [P, 2, 2, P], F32R)
        v_main = m.sb("v_main", [P, NQ, P])
        v_last = m.sb("v_last", [P, NQ, P])
        e = m.sb("e", [P, 2, 2, S])
        a_t = m.sb("a_t", [P, 2, NQ, TB])
        bias = m.sb("bias", [P, STRIP], F16)
        ident = m.sb("ident", [P, P])
        ones = m.sb("ones", [P, P])
        att = m.sb("att", [P, 2, TB])
        att_sq = m.sb("att_sq", [P, TB])
        total = m.sb("total", [P, TB])
        top = m.sb("top", [P, 2, 2, 2])
        neg_top = m.sb("neg_top", [P, 2, 2])
        esum = m.sb("esum", [P, 2, 2])
        coef = m.sb("coef", [P, 2])
        eps_sum = m.sb("eps_sum", [P, NQ])
        lam_v = m.sb("lam_v", [P, 4, DH])
        lam_p = m.sb("lam_p", [P, DH])
        lam_e = m.sb("lam_e", [P, 4])
        neg_lam = m.sb("neg_lam", [P, 1])
        score = m.ps("score", [P, 2, HALF])
        turned = m.ps("turned", [P, 2, TB])
        pv = m.ps("pv", [P, TB])
        stat = m.ps("stat", [P, TB])

        lam_loaded = m.sem("lam_loaded")
        lam_step = m.sem("lam_step")
        lam_exp = m.sem("lam_exp")
        consts_step = m.sem("consts_step")
        distance_ready = m.sem("distance_ready")
        bias_ready = m.sem("bias_ready")
        waited = m.sem("waited")
        k_loaded = m.sem("k_loaded")
        v_main_loaded = m.sem("v_main_loaded")
        v_last_loaded = m.sem("v_last_loaded")
        q_loaded = [m.sem(f"q_loaded{i}") for i in range(4)]
        k_hi_ready = m.sem("k_hi_ready")
        k_lo_ready = m.sem("k_lo_ready")
        q_hi_ready = m.sem("q_hi_ready")
        q_lo_ready = m.sem("q_lo_ready")
        scores_done = m.sem("scores_done")
        biased = m.sem("biased")
        neg_top_ready = m.sem("neg_top_ready")
        exp_done = m.sem("exp_done")
        coef_step = m.sem("coef_step")
        combined = m.sem("combined")
        turned_done = m.sem("turned_done")
        turned_out = m.sem("turned_out")
        pv_done = m.sem("pv_done")
        pv_out = m.sem("pv_out")
        att_sq_ready = m.sem("att_sq_ready")
        stat_done = m.sem("stat_done")
        stat_out = m.sem("stat_out")
        att_stored = [m.sem("att_stored0"), m.sem("att_stored1")]
        total_stored = m.sem("total_stored")
        block = ctx.enter_context(nc.Block())

        def static(x):
            return isinstance(x, int)

        def wait(eng, sem, value):
            if not static(value) or value > 0:
                eng.wait_ge(sem, value)

        def due(h, s, at):
            b = (s - at) // QB
            if (s - at) % QB or (static(h) and h * NB + b < 0):
                return None
            if static(h) and h * NB + b >= H * NB:
                return None
            return b

        @block.sync
        def _(sp):
            sp.dma_start(lam_v[:], lam_in).then_inc(lam_loaded, 16)

            def load_q(h, s):
                n = h * NQ + s
                wait(sp, q_lo_ready, n - 3)
                src = qk_s[bass.ds(h, 1), :, s * P:(s + 1) * P].rearrange("o (c d) t -> (o d) c t", c=2)
                for twin in range(2):
                    sp.dma_start(q_raw[twin * DH:(twin + 1) * DH, s % 4], src).then_inc(q_loaded[s % 4], 16)

            def load_k(h):
                wait(sp, k_lo_ready, 8 * h)
                src = qk_s[bass.ds(h + H, 1)].rearrange("o (c d) t -> (o d) c t", c=2)
                for twin in range(2):
                    sp.dma_start(k_raw[twin * DH:(twin + 1) * DH], src).then_inc(k_loaded, 16)

            def load_v(h, dst, sem):
                src = v_s[:, bass.ds(h * P, P)].rearrange("(k p) c -> p k c", p=P)
                sp.dma_start(dst[:], src).then_inc(sem, 16)

            def store(h, s):
                b = due(h, s, 9 + 4)
                if b is not None:
                    g = h * NB + b
                    sp.wait_ge(pv_out, g + 1)
                    hb = h if b >= 0 else h - 1
                    sp.dma_start(att_s[bass.ds(hb, 1), :, (b % NB) * TB:(b % NB + 1) * TB].rearrange("o p t -> (o p) t"),
                                 att[:, b % 2]).then_inc(att_stored[b % 2], 16)
                b = due(h, s, 11 + 4)
                if b is not None:
                    g = h * NB + b
                    sp.wait_ge(stat_out, g + 1)
                    hb = h if b >= 0 else h - 1
                    sp.dma_start(total_s[bass.ds(hb, 1), :, (b % NB) * TB:(b % NB + 1) * TB].rearrange("o p t -> (o p) t"),
                                 total[:]).then_inc(total_stored, 16)

            def head(h):
                load_k(h)
                for s in range(NQ):
                    load_q(h, s)
                    if s == 1:
                        wait(sp, pv_done, h * NB - 1)
                        load_v(h, v_main, v_main_loaded)
                    if s == 8:
                        wait(sp, pv_done, h * NB)
                        load_v(h, v_last, v_last_loaded)
                    store(h, s)

            head(0)
            with sp.Fori(1, H) as h:
                head(h)
            for s in range(QB * 4):
                store(H, s)
            for i in range(2):
                sp.wait_ge(att_stored[i], 16 * H * NB // 2)
            sp.wait_ge(total_stored, 16 * H * NB)

        @block.gpsimd
        def _(pool):
            pool.memset(ident[:], 0.0).then_inc(consts_step, 1)
            pool.memset(ones[:], 1.0).then_inc(consts_step, 1)
            distance = e[:].rearrange("p a c t -> p (a c t)")[:, 0:STRIP].bitcast(I32)
            pool.iota(distance, pattern=[[-STEP0, STRIP]], base=STEP0 * CENTER, channel_multiplier=STEP0).then_inc(distance_ready, 1)
            pool.wait_ge(consts_step, 2)
            pool.affine_select(out=ident[:], in_=ident[:], compare_op=ALU.not_equal, fill=1.0, base=0,
                               pattern=[[-1, P]], channel_multiplier=1).then_inc(consts_step, 1)
            with pool.Fori(0, H * NB // 2) as pair:
                for slot in range(2):
                    g = pair * 2 + slot
                    pool.wait_ge(pv_out, g + 1)
                    pool.tensor_tensor(att_sq[:], att[:, slot], att[:, slot], ALU.mult).then_inc(att_sq_ready, 1)
                    pool.wait_ge(stat_done, g + 1)

        @block.scalar
        def _(act):
            def q_high(h, s):
                n = h * NQ + s
                act.wait_ge(q_loaded[s % 4], 32 * (h * (NQ // 4) + s // 4 + 1))
                wait(act, scores_done, 4 * (n - 1))
                act.activation(q_hl[:, s % 2], q_raw[:, s % 4], ACT.Copy).then_inc(q_hi_ready, 1)

            def k_high(h):
                act.wait_ge(k_loaded, 32 * (h + 1))
                wait(act, scores_done, 4 * NQ * h)
                for c in range(2):
                    for quarter in range(4):
                        cols = bass.ts(quarter, TB)
                        act.activation(k_hi[:, c, cols], k_raw[:, c, cols], ACT.Copy).then_inc(k_hi_ready, 1)

            def exponential(h, s, c):
                n = h * NQ + s
                act.wait_ge(neg_top_ready, 2 * n + c + 1)
                act.activation(e[:, s % 2, c], e[:, s % 2, c], ACT.Exp, bias=neg_top[:, s % 2, c:c + 1], scale=SCALE,
                               accum_out=esum[:, s % 2, c:c + 1]).then_inc(exp_done, 1)

            def copy_turned(h, s):
                n = h * NQ + s
                if static(n) and n == 0:
                    return
                b, col = (s - 1) // QB, (s - 1) % QB
                if col == 0:
                    wait(act, pv_done, h * NB + b - 1)
                for j in range(4):
                    act.wait_ge(turned_done, 4 * (n - 1) + j + 1)
                    act.activation(a_t[:, b % 2, 4 * j:4 * j + 4, col * P:(col + 1) * P],
                                   turned[:, j % 2].rearrange("p (k q) -> p k q", q=P), ACT.Copy).then_inc(turned_out, 1)

            def copy_results(h, s):
                b = due(h, s, 9)
                if b is not None:
                    g = h * NB + b
                    act.wait_ge(pv_done, g + 1)
                    wait(act, att_stored[b % 2], 16 * (h * (NB // 2) + b // 2))
                    wait(act, att_sq_ready, g - 1)
                    act.activation(att[:, b % 2], pv[:], ACT.Copy).then_inc(pv_out, 1)
                b = due(h, s, 11)
                if b is not None:
                    g = h * NB + b
                    act.wait_ge(stat_done, g + 1)
                    wait(act, total_stored, 16 * g)
                    act.activation(total[:], stat[:], ACT.Copy).then_inc(stat_out, 1)

            def head(h):
                q_high(h, 0)
                k_high(h)
                for s in range(NQ):
                    copy_results(h, s)
                    exponential(h, s, 0)
                    copy_turned(h, s)
                    exponential(h, s, 1)
                    if s + 1 < NQ:
                        q_high(h, s + 1)

            act.wait_ge(lam_step, 2)
            act.activation(lam_e[:, 2:4], lam_e[:, 0:2], ACT.Exp).then_inc(lam_exp, 1)
            head(0)
            with act.Fori(1, H) as h:
                head(h)
            copy_turned(H, 0)
            for s in range(3 * QB):
                copy_results(H, s)

        @block.vector
        def _(dve):
            def q_low(h, s):
                n = h * NQ + s
                dve.wait_ge(q_hi_ready, n + 1)
                low = q_hl[DH:P, s % 2]
                dve.tensor_tensor(low, q_raw[DH:P, s % 4], low.bitcast(F32), ALU.subtract).then_inc(q_lo_ready, 1)

            def k_low(h):
                for c in range(2):
                    for quarter in range(4):
                        dve.wait_ge(k_hi_ready, 8 * h + 4 * c + quarter + 1)
                        cols = bass.ts(quarter, TB)
                        dve.tensor_tensor(k_lo[:, c, cols], k_raw[:, c, cols], k_hi[:, c, cols].bitcast(F32),
                                          ALU.subtract).then_inc(k_lo_ready, 1)

            def add_bias(h, s, c):
                n = h * NQ + s
                if c == 0:
                    wait(dve, turned_done, 4 * (n - 1))
                for half in range(2):
                    hf = 2 * c + half
                    dve.wait_ge(scores_done, 4 * n + hf + 1)
                    if half:
                        dve.wait_ge(biased, 4 * n + hf)
                    dve.sem_inc(waited, 1)
                    at = CENTER - s * P + half * HALF
                    dve.tensor_tensor_reduce(
                        out=e[:, s % 2, c, half * HALF:(half + 1) * HALF], in0=score[:, half], in1=bias[:, at:at + HALF],
                        scale=1.0, scalar=top[:, s % 2, c, 0:1] if half else -3.0e38, op0=ALU.add, op1=ALU.max,
                        accum_out=top[:, s % 2, c, half:half + 1]).then_inc(biased, 1)
                dve.wait_ge(biased, 4 * n + 2 * c + 2)
                dve.tensor_scalar(neg_top[:, s % 2, c:c + 1], top[:, s % 2, c, 1:2], -SCALE, None, ALU.mult)\
                    .then_inc(neg_top_ready, 1)

            def combine(h, s):
                n = h * NQ + s
                if static(n) and n == 0:
                    return
                slot = (s - 1) % 2
                dve.wait_ge(exp_done, 2 * n)
                if (s - 1) % QB == 0:
                    wait(dve, stat_done, h * NB + (s - 1) // QB - NB + 1)
                at = (s - 1) % NQ
                dve.reciprocal(coef[:, 0:1], esum[:, slot, 1:2]).then_inc(coef_step, 1)
                dve.scalar_tensor_tensor(eps_sum[:, at:at + 1], esum[:, slot, 0:1], P * EPS, esum[:, slot, 0:1],
                                         ALU.mult, ALU.mult)
                dve.wait_ge(coef_step, 2 * n - 1)
                dve.scalar_tensor_tensor(coef[:, 1:2], esum[:, slot, 0:1], neg_lam[:, 0:1], coef[:, 0:1],
                                         ALU.mult, ALU.mult).then_inc(coef_step, 1)
                dve.wait_ge(coef_step, 2 * n)
                dve.scalar_tensor_tensor(e[:, slot, 0], e[:, slot, 1], coef[:, 1:2], e[:, slot, 0],
                                         ALU.mult, ALU.add).then_inc(combined, 1)

            def head(h):
                if not static(h):
                    dve.tensor_scalar(bias[:], bias[:], 0.25, None, ALU.mult).then_inc(bias_ready, 1)
                q_low(h, 0)
                k_low(h)
                dve.wait_ge(bias_ready, h + 1)
                for s in range(NQ):
                    add_bias(h, s, 0)
                    combine(h, s)
                    add_bias(h, s, 1)
                    if s + 1 < NQ:
                        q_low(h, s + 1)

            dve.wait_ge(lam_loaded, 16)
            for i in range(2):
                if i:
                    dve.wait_ge(lam_step, 1)
                dve.tensor_tensor_reduce(out=lam_p[:], in0=lam_v[:, 2 * i], in1=lam_v[:, 2 * i + 1], scale=1.0, scalar=0.0,
                                         op0=ALU.mult, op1=ALU.add, accum_out=lam_e[:, i:i + 1]).then_inc(lam_step, 1)
            dve.wait_ge(distance_ready, 1)
            distance = e[:].rearrange("p a c t -> p (a c t)")[:, 0:STRIP].bitcast(I32)
            dve.scalar_tensor_tensor(bias[:], distance, -1.0, distance, ALU.mult, ALU.min).then_inc(bias_ready, 1)
            dve.wait_ge(lam_exp, 1)
            dve.tensor_tensor(neg_lam[:], lam_e[:, 3:4], lam_e[:, 2:3], ALU.subtract).then_inc(lam_step, 1)
            dve.wait_ge(lam_step, 3)
            dve.tensor_scalar(neg_lam[:], neg_lam[:], LAM_INIT, None, ALU.subtract).then_inc(lam_step, 1)
            dve.wait_ge(lam_step, 4)
            head(0)
            with dve.Fori(1, H) as h:
                head(h)
            combine(H, 0)

        @block.tensor
        def _(pe):
            def scores(h, s, hf):
                n = h * NQ + s
                c, half = hf // 2, hf % 2
                if hf == 0:
                    pe.wait_ge(q_lo_ready, n + 1)
                if s == 0:
                    pe.wait_ge(k_lo_ready, 8 * h + 2 * (hf + 1))
                wait(pe, biased, 4 * n + hf - 1)
                for bank in range(HALF // TB):
                    cols = slice(half * HALF + bank * TB, half * HALF + (bank + 1) * TB)
                    out = score[:, half, bank * TB:(bank + 1) * TB]
                    pe.matmul(out, q_hl[:, s % 2, c], k_hi[:, c, cols], start=True, stop=False)
                    last = pe.matmul(out, q_hl[:, s % 2, c], k_lo[:, c, cols], start=False, stop=True)
                last.then_inc(scores_done, 1)

            def values(h, s, part):
                b, j = (s - 5) // QB, (s - 5) % QB
                if static(h) and not 0 <= h * NB + b < H * NB:
                    return
                g = h * NB + b
                if j == 0 and part == 0:
                    pe.wait_ge(turned_out, 16 * (g + 1))
                    wait(pe, pv_out, g)
                    if b == -1:
                        pe.wait_ge(v_last_loaded, 16 * h)
                    if b == 0:
                        pe.wait_ge(v_main_loaded, 16 * (h + 1))
                v = v_last if b == -1 else v_main
                for i in range(2):
                    kt = 4 * j + 2 * part + i
                    last = pe.matmul(pv[:], v[:, kt], a_t[:, b % 2, kt], start=(kt == 0), stop=(kt == NQ - 1))
                if kt == NQ - 1:
                    last.then_inc(pv_done, 1)

            def turn(h, s, j):
                n = h * NQ + s
                if static(n) and n == 0:
                    return
                if j == 0:
                    pe.wait_ge(combined, n)
                wait(pe, turned_out, 4 * (n - 1) + j - 1)
                for i in range(4):
                    kt = 4 * j + i
                    last = pe.transpose(turned[:, j % 2, i * P:(i + 1) * P], e[:, (s - 1) % 2, 0, kt * P:(kt + 1) * P],
                                        ident[:])
                last.then_inc(turned_done, 1)

            def statistics(h, s):
                b = due(h, s, 10)
                if b is None:
                    return
                g = h * NB + b
                pe.wait_ge(att_sq_ready, g + 1)
                wait(pe, stat_out, g)
                for c in range(QB):
                    at = (b % NB) * QB + c
                    pe.matmul(stat[:, c * P:(c + 1) * P], eps_sum[:, at:at + 1].to_broadcast([P, P]), ident[:],
                              start=(c == 0), stop=False, skip_group_check=True)
                last = pe.matmul(stat[:], ones[:], att_sq[:], start=False, stop=True, skip_group_check=True)
                last.then_inc(stat_done, 1)

            def step(h, s):
                scores(h, s, 0)
                scores(h, s, 1)
                values(h, s, 0)
                scores(h, s, 2)
                scores(h, s, 3)
                turn(h, s, 0)
                turn(h, s, 1)
                values(h, s, 1)
                turn(h, s, 2)
                turn(h, s, 3)
                statistics(h, s)

            pe.wait_ge(consts_step, 3)
            for s in range(NQ):
                step(0, s)
            with pe.Fori(1, H) as h:
                for s in range(NQ):
                    step(h, s)
            for j in range(4):
                turn(H, 0, j)
            for s in range(3 * QB):
                values(H, s, 0)
                values(H, s, 1)
                statistics(H, s)


def phase_ssm(nc, s_par, s_d, s_bc, w_glu, b_glu, u_s, ssm_s):
    T = 8
    NJ = S // T
    G = 8
    GH = 16
    PAIRS = 2 * G
    NQU = 4
    N = 64
    NDG = NQU * PAIRS
    JB = NJ // P
    BATCH = 2
    XR = 6
    MAG, THETA, A_RE, A_IM, E_RE, E_IM, NPAR = 0, 1, 2, 2 + T + 1, 4 + 2 * T, 4 + 3 * T, 4 + 4 * T
    MAGIC = 1.5 * 2.0 ** 23
    TURN = 2.0 * math.pi
    C1 = 6.28125
    C2 = float(np.float32(math.floor((TURN - C1) * 2.0 ** 22) / 2.0 ** 22))
    C3 = float(np.float32(TURN - C1 - C2))
    PI_BELOW = 3.1415925
    with ExitStack() as ctx:
        m = Memory(nc, ctx, "sm")
        par = m.sb("par", [P, NPAR, NDG])
        par_q = m.sb("par_q", [P, NPAR, PAIRS])
        bc = m.sb("bc", [P, 4, PAIRS, GH])
        bp = m.sb("bp", [P, PAIRS, T, GH])
        cp = m.sb("cp", [P, PAIRS, T + 1, GH])
        cp_swap = m.sb("cp_swap", [P, PAIRS, T + 1, GH])
        part = m.sb("part", [P, PAIRS, T + 1, GH])
        strip = m.sb("strip", [GH, G, 2 * T - 1, GH])
        toeplitz = m.sb("toeplitz", [P, G, P])
        p_t = m.sb("p_t", [P, PAIRS, 3 * N])
        u_raw = m.sb("u_raw", [P, JB, T, P])
        uz = m.sb("uz", [P, JB, T * P])
        u_t = m.sb("u_t", [P, G, NJ])
        tab = m.sb("tab", [P, PAIRS, 2, NJ])
        cycles = m.sb("cycles", [P, BATCH, NJ])
        whole = m.sb("whole", [P, BATCH, NJ])
        half_sine = m.sb("half_sine", [P, 2, BATCH, NJ])
        turned_w = m.sb("turned_w", [P, 2, 2, NJ])
        scan_in = m.sb("scan_in", [P, 2, NJ])
        scan_out = m.sb("scan_out", [P, 2, NJ])
        x_st = m.sb("x_st", [P, XR, 2, NJ + 1])
        z_t = m.sb("z_t", [P, NQU, S])
        wg = m.sb("wg", [P, 4, ATT])
        bg = m.sb("bg", [P, 4])
        chunk_i = m.sb("chunk_i", [P, NJ], I32)
        chunk = m.sb("chunk", [P, NJ])
        sign = m.sb("sign", [P, 3])
        ident = m.sb("ident", [P, P])
        d_in = m.sb("d_in", [GH, NDG // 2])
        d_diag = m.sb("d_diag", [GH, NDG // 2, GH])
        d_q = m.sb("d_q", [GH, G, GH])
        gate = tab[:].rearrange("p a c t -> p (a c t)")[:, 0:2 * TB].rearrange("p (r t) -> p r t", r=2)
        out = tab[:].rearrange("p a c t -> p (a c t)")[:, 2 * TB:4 * TB].rearrange("p (r t) -> p r t", r=2)
        w_ps = m.ps("w_ps", [P, 2, 2, NJ])
        y_ps = m.ps("y_ps", [P, 2, TB])
        turn_ps = m.ps("turn_ps", [P, 2, TB])
        lag_ps = m.ps("lag_ps", [P, 2, TB])

        const_loaded = m.sem("const_loaded")
        const_step = m.sem("const_step")
        prep = m.sem("prep")
        prep_act = m.sem("prep_act")
        waited = m.sem("waited")
        bc_loaded = m.sem("bc_loaded")
        u_loaded = m.sem("u_loaded")
        ug_ready = m.sem("ug_ready")
        par_q_ready = m.sem("par_q_ready")
        product_step = m.sem("product_step")
        bp_ready = m.sem("bp_ready")
        cp_ready = m.sem("cp_ready")
        swap_loaded = m.sem("swap_loaded")
        lag_done = m.sem("lag_done")
        strip_step = m.sem("strip_step")
        strip_ready = m.sem("strip_ready")
        toeplitz_loaded = m.sem("toeplitz_loaded")
        turn_done = m.sem("turn_done")
        turn_out = m.sem("turn_out")
        phase_step = m.sem("phase_step")
        cycles_ready = m.sem("cycles_ready")
        sines_ready = m.sem("sines_ready")
        tab_ready = m.sem("tab_ready")
        w_done = m.sem("w_done")
        turned_ready = m.sem("turned_ready")
        scan_in_ready = m.sem("scan_in_ready")
        scanned = m.sem("scanned")
        x_ready = m.sem("x_ready")
        ug_half = m.sem("ug_half")
        p_half = m.sem("p_half")
        bc_signed = m.sem("bc_signed")
        phase_act = m.sem("phase_act")
        cosine_step = m.sem("cosine_step")
        edges_ready = m.sem("edges_ready")
        y_done = m.sem("y_done")
        z_ready = m.sem("z_ready")
        glu_done = m.sem("glu_done")
        gate_ready = m.sem("gate_ready")
        out_ready = m.sem("out_ready")
        out_stored = [m.sem("out_stored0"), m.sem("out_stored1")]
        block = ctx.enter_context(nc.Block())

        DT, LR, ANG, MG, MG8, KK, RR, SN, SH, TH, NR, DEN, CR, CI, NCOL = range(15)
        PREP_LR, PREP_R, PREP_END = 2, 8, 68

        def scr(t, i, n=1):
            flat = t[:].rearrange("p a c t -> p (a c t)")[:, i * NDG:(i + n) * NDG]
            return flat if n == 1 else flat.rearrange("p (n d) -> p n d", n=n)

        def scr_block(t, i, a, n):
            return scr(t, i, a * n).rearrange("p (a n) d -> p a n d", a=a)

        def pair(i):
            return (i % 2) * G + i // 2

        def x_slot(i):
            return i % XR

        U_TURNS, B_TURNS, Z_TURNS = 4, 4, 4
        QT = U_TURNS + B_TURNS + Z_TURNS
        u_chunks = u_s.rearrange("(b j s) c -> j b s c", b=JB, s=T)
        first_chunk = uz[:].rearrange("p b (s c) -> p b s c", s=T)

        def static(x):
            return isinstance(x, int)

        def wait(eng, sem, value):
            if not static(value) or value > 0:
                eng.wait_ge(sem, value)

        def quarters(eng, body):
            body(0)
            with eng.Fori(1, NQU) as q:
                body(q)

        @block.sync
        def _(sp):
            sp.dma_start(par[:, 0:3], s_par).then_inc(const_loaded, 16)
            sp.dma_start(d_in[:], s_d).then_inc(const_loaded, 16)
            sp.dma_start(bg[:], b_glu).then_inc(const_loaded, 16)
            sp.dma_start(wg[:], w_glu).then_inc(const_loaded, 16)

            def body(q):
                wait(sp, cp_ready, q)
                sp.dma_start(bc[:], s_bc[bass.ds(q, 1)].rearrange("o p a b c -> (o p) a b c")).then_inc(bc_loaded, 16)
                wait(sp, ug_ready, q)
                for b in range(JB):
                    sp.dma_start(u_raw[:, b], u_chunks[:, b, :, bass.ds(q * P, P)]).then_inc(u_loaded, 16)
                wait(sp, y_done, q * G)
                sp.sem_inc(waited, 1)
                sp.wait_ge(cp_ready, q + 1)
                for h in range(2):
                    sp.dma_start(cp_swap[(1 - h) * N:(2 - h) * N], cp[h * N:(h + 1) * N]).then_inc(swap_loaded, 16)
                sp.wait_ge(strip_ready, q + 1)
                for s in range(T):
                    sp.dma_start(toeplitz[s * GH:(s + 1) * GH].rearrange("p g (s h) -> p g s h", s=T),
                                 strip[:, :, T - 1 - s:2 * T - 1 - s]).then_inc(toeplitz_loaded, 16)

            quarters(sp, body)
            for n in range(4 * NTB):
                tb, c = n // 4, n % 4
                sp.wait_ge(out_ready, n + 1)
                sp.dma_start(ssm_s[c, :, tb * TB:(tb + 1) * TB], out[:, n % 2]).then_inc(out_stored[n % 2], 16)
            for i in range(2):
                sp.wait_ge(out_stored[i], 16 * 2 * NTB)

        @block.gpsimd
        def _(pool):
            pool.memset(ident[:], 0.0).then_inc(const_step, 1)
            pool.iota(chunk_i[:], pattern=[[1, NJ]], base=0, channel_multiplier=0).then_inc(const_step, 1)
            for h, s in ((0, 1.0), (1, -1.0)):
                rows = slice(h * N, (h + 1) * N)
                pool.wait_ge(const_step, 2 + 2 * h)
                pool.memset(sign[rows, 0:1], s).then_inc(const_step, 1)
                pool.memset(sign[rows, 1:2], s * 2 * PI_BELOW).then_inc(const_step, 1)
            pool.wait_ge(const_step, 6)
            pool.affine_select(out=ident[:], in_=ident[:], compare_op=ALU.not_equal, fill=1.0, base=0,
                               pattern=[[-1, P]], channel_multiplier=1).then_inc(const_step, 1)
            pool.tensor_copy(chunk[:], chunk_i[:]).then_inc(const_step, 1)

        @block.scalar
        def _(act):
            def turn_end(q, turn):
                act.wait_ge(turn_done, q * QT + turn + 1)
                act.sem_inc(waited, 1)

            act.wait_ge(const_loaded, 64)
            act.activation(scr(tab, DT), par[:, 2], ACT.Exp).then_inc(prep_act, 1)
            act.wait_ge(prep, PREP_LR)
            act.activation(scr(tab, MG), scr(tab, LR), ACT.Exp)
            act.activation(scr(tab, MG8), scr(tab, LR), ACT.Exp, scale=float(T)).then_inc(prep_act, 1)
            act.wait_ge(prep, PREP_R)
            act.activation(scr(tab, SN), scr(tab, RR), ACT.Sin)
            act.activation(scr(tab, SH), scr(tab, RR), ACT.Sin, scale=0.5).then_inc(prep_act, 1)

            def body(q):
                act.wait_ge(u_loaded, 16 * JB * (q + 1))
                wait(act, turn_done, q * QT)
                for b in range(JB):
                    act.activation(uz[:, b].rearrange("p (g s h) -> p s g h", g=G, s=T),
                                   u_raw[:, b].rearrange("p s (g h) -> p s g h", g=G), ACT.Copy).then_inc(ug_half, 1)
                act.wait_ge(ug_half, JB * (q + 1))
                act.sem_inc(ug_ready, 1)
                wait(act, y_done, q * G)
                for t in range(U_TURNS):
                    turn_end(q, t)
                    act.activation(u_t[:, 2 * t:2 * t + 2], turn_ps[:, t % 2].rearrange("p (g j) -> p g j", g=2),
                                   ACT.Copy).then_inc(turn_out, 1)
                for t in range(B_TURNS):
                    turn_end(q, U_TURNS + t)
                    src = turn_ps[:, t % 2].rearrange("p (g n) -> p g n", g=4)
                    act.activation(p_t[:, 4 * t:4 * t + 4, 0:P], src, ACT.Copy).then_inc(p_half, 1)
                    act.activation(p_t[:, 4 * t:4 * t + 4, P:3 * N], src[:, :, 0:N], ACT.Copy).then_inc(p_half, 1)
                    act.wait_ge(p_half, q * 2 * B_TURNS + 2 * t + 2)
                    act.sem_inc(turn_out, 1)
                if static(q):
                    act.wait_ge(prep, PREP_END)
                wait(act, x_ready, q * PAIRS)
                for b in range(PAIRS // BATCH):
                    act.wait_ge(cycles_ready, q * (PAIRS // BATCH) + b + 1)
                    hs = half_sine[:, b % 2]
                    act.activation(hs, cycles[:], ACT.Sin, scale=PI_BELOW).then_inc(phase_act, 1)
                    act.activation(tab[:, b * BATCH:(b + 1) * BATCH, 1], cycles[:], ACT.Sin, scale=sign[:, 1:2])\
                        .then_inc(sines_ready, 1)
                for g in range(G):
                    act.wait_ge(y_done, q * G + g + 1)
                    act.activation(first_chunk[:, :, :, g * GH:(g + 1) * GH],
                                   y_ps[:, g % 2, 0:JB * P].rearrange("p (b s h) -> p b s h", b=JB, s=T),
                                   ACT.Gelu).then_inc(z_ready, 1)
                for t in range(Z_TURNS):
                    turn_end(q, U_TURNS + B_TURNS + t)
                    b, s4 = t // 2, t % 2
                    dst = z_t[:, bass.ds(q, 1)].rearrange("p o (b j s) -> p (o b) s j", b=JB, s=T)
                    act.activation(dst[:, b, 4 * s4:4 * s4 + 4], turn_ps[:, t % 2].rearrange("p (s j) -> p s j", s=4),
                                   ACT.Copy).then_inc(turn_out, 1)

            quarters(act, body)
            for n in range(4 * NTB):
                act.wait_ge(glu_done, n + 1)
                wait(act, out_ready, n - 1)
                act.activation(gate[:, n % 2], y_ps[:, n % 2], ACT.Sigmoid, bias=bg[:, n % 4:n % 4 + 1])\
                    .then_inc(gate_ready, 1)

        @block.vector
        def _(dve):
            steps = [0]

            def then(instruction):
                instruction.then_inc(prep, 1)
                steps[0] += 1
                dve.wait_ge(prep, steps[0])

            def col(i):
                return scr(tab, i)

            def tt(o, a, b, op):
                then(dve.tensor_tensor(o, a, b, op))

            def reduce(r, x, k, inv_period, c1, c2, c3):
                then(dve.tensor_scalar(k, x, inv_period, MAGIC, ALU.mult, ALU.add))
                then(dve.tensor_scalar(k, k, MAGIC, None, ALU.subtract))
                then(dve.scalar_tensor_tensor(r, k, -c1, x, ALU.mult, ALU.add))
                then(dve.scalar_tensor_tensor(r, k, -c2, r, ALU.mult, ALU.add))
                then(dve.scalar_tensor_tensor(r, k, -c3, r, ALU.mult, ALU.add))

            def complex_mult(o_re, o_im, a_re, a_im, b_re, b_im, tmp):
                tt(tmp, a_im, b_im, ALU.mult)
                tt(o_re, a_re, b_re, ALU.mult)
                tt(o_re, o_re, tmp, ALU.subtract)
                tt(tmp, a_im, b_re, ALU.mult)
                tt(o_im, a_re, b_im, ALU.mult)
                tt(o_im, o_im, tmp, ALU.add)

            def parameters():
                re, im = par[:, 0], par[:, 1]
                dve.wait_ge(const_loaded, 64)
                dve.wait_ge(prep_act, 1)
                tt(col(LR), re, col(DT), ALU.mult)
                tt(col(ANG), im, col(DT), ALU.mult)
                assert steps[0] == PREP_LR
                reduce(col(RR), col(ANG), col(KK), 1.0 / TURN, C1, C2, C3)
                then(dve.tensor_scalar(col(RR), col(RR), PI_BELOW, -PI_BELOW, ALU.min, ALU.max))
                assert steps[0] == PREP_R
                reduce(col(TH), col(RR), col(KK), T / TURN, C1 / T, C2 / T, C3 / T)
                then(dve.tensor_scalar(col(TH), col(TH), T / TURN, None, ALU.mult))
                dve.wait_ge(prep_act, 3)
                powers, inputs = scr_block(tab, NCOL, 2, T + 1), scr_block(tab, NCOL + 2 * T + 2, 2, T)
                tmp = scr_block(tab, NCOL + 4 * T + 2, 1, T)[:, 0]
                then(dve.scalar_tensor_tensor(col(KK), col(SH), -2.0, col(SH), ALU.mult, ALU.mult))
                then(dve.tensor_scalar(col(KK), col(KK), 1.0, None, ALU.add))
                tt(powers[:, 0, 1], col(KK), col(MG), ALU.mult)
                tt(powers[:, 1, 1], col(SN), col(MG), ALU.mult)
                then(dve.memset(powers[:, 0, 0], 1.0))
                then(dve.memset(powers[:, 1, 0], 0.0))
                for have in (1, 2, 4):
                    a, b = powers[:, :, have], powers[:, :, 1:have + 1]
                    o = powers[:, :, have + 1:2 * have + 1]
                    by = [a[:, i].unsqueeze(1).to_broadcast([P, have, NDG]) for i in range(2)]
                    complex_mult(o[:, 0], o[:, 1], by[0], by[1], b[:, 0], b[:, 1], tmp[:, 0:have])
                ar, ai = powers[:, 0, 1], powers[:, 1, 1]
                then(dve.tensor_scalar(col(NR), ar, 1.0, None, ALU.subtract))
                tt(col(KK), re, re, ALU.mult)
                tt(col(DEN), im, im, ALU.mult)
                tt(col(DEN), col(DEN), col(KK), ALU.add)
                then(dve.reciprocal(col(DEN), col(DEN)))
                tt(col(CR), col(NR), re, ALU.mult)
                tt(col(KK), ai, im, ALU.mult)
                tt(col(CR), col(CR), col(KK), ALU.add)
                tt(col(CR), col(CR), col(DEN), ALU.mult)
                tt(col(CI), ai, re, ALU.mult)
                tt(col(KK), col(NR), im, ALU.mult)
                tt(col(CI), col(CI), col(KK), ALU.subtract)
                tt(col(CI), col(CI), col(DEN), ALU.mult)
                cr, ci = (col(i).unsqueeze(1).to_broadcast([P, T, NDG]) for i in (CR, CI))
                complex_mult(inputs[:, 0], inputs[:, 1], cr, ci, powers[:, 0, 0:T], powers[:, 1, 0:T], tmp)
                then(dve.tensor_copy(par[:, MAG], col(MG8)))
                then(dve.tensor_copy(par[:, THETA], col(TH)))
                for src, to, n, flipped in ((powers, (A_RE, A_IM), T + 1, 1), (inputs, (E_RE, E_IM), T, 0)):
                    for ri in range(2):
                        dst = par[:, to[ri]:to[ri] + n].rearrange("p n (q d g) -> p n q d g", q=NQU, d=2)
                        s = src[:, ri].rearrange("p n (q d g) -> p n q d g", q=NQU, d=2)
                        for d in range(2):
                            sd = s[:, ::-1, :, d] if d == flipped else s[:, :, :, d]
                            then(dve.tensor_copy(dst[:, :, :, d], sd))
                then(dve.tensor_tensor(d_diag[:], ident[0:GH, 0:GH].unsqueeze(1).to_broadcast([GH, NDG // 2, GH]),
                                       d_in[:].unsqueeze(2).to_broadcast([GH, NDG // 2, GH]), ALU.mult))
                assert steps[0] == PREP_END, steps[0]

            def outer(q, dst, re, im, n, src, nth):
                shape = [P, PAIRS, n, GH]

                def coef(i):
                    return par_q[:, i:i + n].rearrange("p n d -> p d n").unsqueeze(3).to_broadcast(shape)

                dve.tensor_tensor(dst, coef(re), bc[:, src].unsqueeze(2).to_broadcast(shape), ALU.mult)\
                    .then_inc(product_step, 1)
                dve.tensor_tensor(part[:, :, 0:n], coef(im), bc[:, src + 1].unsqueeze(2).to_broadcast(shape), ALU.mult)\
                    .then_inc(product_step, 1)
                dve.wait_ge(product_step, q * 4 + 2 * nth + 2)
                return dve.tensor_tensor(dst, dst, part[:, :, 0:n], ALU.subtract)

            def make_cycles(q, b):
                n = q * (PAIRS // BATCH) + b
                wait(dve, sines_ready, n)
                shape = [P, BATCH, NJ]
                dve.tensor_tensor(cycles[:], chunk[:].unsqueeze(1).to_broadcast(shape),
                                  par_q[:, THETA, b * BATCH:(b + 1) * BATCH].unsqueeze(2).to_broadcast(shape),
                                  ALU.mult).then_inc(phase_step, 1)
                dve.wait_ge(phase_step, 2 * n + 1)
                dve.tensor_scalar(whole[:], cycles[:], MAGIC, MAGIC, ALU.add, ALU.subtract).then_inc(phase_step, 1)
                dve.wait_ge(phase_step, 2 * n + 2)
                dve.tensor_tensor(cycles[:], cycles[:], whole[:], ALU.subtract).then_inc(cycles_ready, 1)

            def make_cosines(q, b):
                n = q * (PAIRS // BATCH) + b
                dve.wait_ge(phase_act, n + 1)
                hs = half_sine[:, b % 2]
                dve.scalar_tensor_tensor(hs, hs, -2.0, hs, ALU.mult, ALU.mult).then_inc(cosine_step, 1)
                dve.wait_ge(cosine_step, n + 1)
                dve.tensor_scalar(tab[:, b * BATCH:(b + 1) * BATCH, 0], hs, 1.0, None, ALU.add).then_inc(tab_ready, 1)

            def tables(q, start, stop):
                for b in range(start, stop):
                    make_cycles(q, b)
                    if b:
                        make_cosines(q, b - 1)
                if stop == PAIRS // BATCH:
                    make_cosines(q, stop - 1)

            def make_strip(q, half):
                n = q * 2 + half
                dve.wait_ge(lag_done, n + 1)
                gs = slice(half * 4, half * 4 + 4)
                fwd, bwd = (lag_ps[0:GH, d].rearrange("p (g s h) -> p g s h", g=4, s=T) for d in range(2))
                dve.tensor_copy(strip[:, gs, T - 1:], fwd).then_inc(strip_step, 1)
                dve.tensor_copy(strip[:, gs, 0:T - 1], bwd[:, :, 0:T - 1])
                dve.wait_ge(strip_step, 3 * n + 1)
                mid = strip[:, gs, T - 1]
                dve.tensor_tensor(mid, mid, bwd[:, :, T - 1], ALU.add).then_inc(strip_step, 1)
                dve.wait_ge(strip_step, 3 * n + 2)
                dve.tensor_tensor(mid, mid, d_q[:, gs], ALU.add).then_inc(strip_step, 1)

            def main(q):
                def turn_back(i):
                    n = q * PAIRS + i
                    d = i % 2
                    dve.wait_ge(w_done, n + 1)
                    wait(dve, scan_in_ready, n - 1)
                    w = w_ps[:, i % 2]
                    dve.tensor_tensor(turned_w[:, i % 2], w[:, :, ::-1] if d else w, tab[:, pair(i)], ALU.mult)\
                        .then_inc(turned_ready, 1)

                def add(i):
                    n = q * PAIRS + i
                    dve.wait_ge(turned_ready, n + 1)
                    wait(dve, scanned, n - 1)
                    dve.tensor_tensor(scan_in[:, i % 2], turned_w[:, i % 2, 0], turned_w[:, i % 2, 1], ALU.add)\
                        .then_inc(scan_in_ready, 1)

                def scan(i):
                    n = q * PAIRS + i
                    dve.wait_ge(scan_in_ready, n + 1)
                    wait(dve, x_ready, n - 1)
                    p = pair(i)
                    dve.tensor_tensor_scan(scan_out[:, i % 2], par_q[:, MAG, p:p + 1].to_broadcast([P, NJ]),
                                           scan_in[:, i % 2], 0.0, ALU.mult, ALU.add).then_inc(scanned, 1)

                def turn_forward(i):
                    n = q * PAIRS + i
                    d = i % 2
                    slot = x_slot(i)
                    dve.wait_ge(scanned, n + 1)
                    if i >= XR:
                        dve.wait_ge(y_done, q * G + (i - XR) // 2 + 1)
                    cols = x_st[:, slot, :, 0:NJ] if d else x_st[:, slot, :, 1:NJ + 1]
                    src = scan_out[:, i % 2].unsqueeze(1).to_broadcast([P, 2, NJ])
                    dve.tensor_tensor(cols[:, :, ::-1] if d else cols, src, tab[:, pair(i)], ALU.mult)\
                        .then_inc(x_ready, 1)

                wait(dve, y_done, q * G)
                for i in range(PAIRS + 3):
                    for stage, at in ((turn_back, i), (add, i - 1), (scan, i - 2), (turn_forward, i - 3)):
                        if 0 <= at < PAIRS:
                            stage(at)

            def body(q):
                if not static(q):
                    dve.wait_ge(scanned, q * PAIRS)
                dve.tensor_copy(par_q[:], par[:, :, bass.ds(q * PAIRS, PAIRS)]).then_inc(par_q_ready, 1)
                wait(dve, strip_step, 6 * q)
                dve.tensor_copy(d_q[:], d_diag[:, bass.ds(q * G, G)]).then_inc(par_q_ready, 1)
                dve.wait_ge(par_q_ready, 2 * q + 2)
                dve.wait_ge(bc_loaded, 16 * q + 16)
                for i in (1, 2):
                    dve.tensor_scalar(bc[:, i], bc[:, i], sign[:, 0:1], None, ALU.mult).then_inc(bc_signed, 1)
                dve.wait_ge(bc_signed, 2 * q + 2)
                wait(dve, lag_done, 2 * q)
                wait(dve, cp_ready, q)
                dve.sem_inc(waited, 1)
                outer(q, bp[:], E_RE, E_IM, T, 0, 0).then_inc(bp_ready, 1)
                if static(q):
                    dve.wait_ge(prep, PREP_END)
                tables(q, 0, 4)
                dve.wait_ge(bp_ready, q + 1)
                wait(dve, y_done, q * G)
                wait(dve, swap_loaded, 32 * q)
                dve.sem_inc(waited, 1)
                outer(q, cp[:], A_RE, A_IM, T + 1, 2, 1).then_inc(cp_ready, 1)
                tables(q, 4, 6)
                wait(dve, toeplitz_loaded, 16 * T * q)
                make_strip(q, 0)
                make_strip(q, 1)
                dve.wait_ge(strip_step, 6 * q + 6)
                dve.sem_inc(strip_ready, 1)
                tables(q, 6, PAIRS // BATCH)
                dve.wait_ge(tab_ready, PAIRS // BATCH * (q + 1))
                dve.wait_ge(sines_ready, PAIRS // BATCH * (q + 1))
                main(q)

            dve.wait_ge(const_step, 8)
            parameters()
            for slot in range(XR):
                edge = 0 if slot % 2 == 0 else NJ
                dve.memset(x_st[:, slot, :, edge:edge + 1], 0.0).then_inc(edges_ready, 1)
            quarters(dve, body)
            for n in range(4 * NTB):
                tb, c = n // 4, n % 4
                dve.wait_ge(gate_ready, n + 1)
                if n >= 2:
                    dve.wait_ge(out_stored[n % 2], 16 * (n // 2))
                dve.tensor_tensor(out[:, n % 2], gate[:, n % 2], z_t[:, c, tb * TB:(tb + 1) * TB], ALU.mult)\
                    .then_inc(out_ready, 1)

        @block.tensor
        def _(pe):
            def turn(q, t, sources):
                n = q * QT + t
                wait(pe, turn_out, n - 1)
                for i, src in enumerate(sources):
                    last = pe.transpose(turn_ps[:, t % 2, i * P:(i + 1) * P], src, ident[:])
                last.then_inc(turn_done, 1)

            def lags(q, half):
                wait(pe, strip_step, 6 * q + 3 * half)
                for d in range(2):
                    for g in range(4):
                        p = d * G + half * 4 + g
                        last = pe.matmul(lag_ps[0:GH, d, g * P:(g + 1) * P], bp[:, p, 0 if d else T - 1],
                                         cp[:, p, d:d + T].rearrange("p s h -> p (s h)"), start=True, stop=True)
                last.then_inc(lag_done, 1)

            def main(q):
                def inputs(i):
                    n = q * PAIRS + i
                    wait(pe, turned_ready, n - 1)
                    p, g = pair(i), i // 2
                    pe.matmul(w_ps[:, i % 2, 0], p_t[:, p, 0:P], u_t[:, g], start=True, stop=True)
                    pe.matmul(w_ps[:, i % 2, 1], p_t[:, p, N:3 * N], u_t[:, g], start=True, stop=True)\
                        .then_inc(w_done, 1)

                def outputs(g):
                    n = q * G + g
                    pe.wait_ge(x_ready, q * PAIRS + 2 * g + 2)
                    wait(pe, z_ready, n - 1)
                    if g == 0:
                        pe.wait_ge(swap_loaded, 32 * (q + 1))
                        pe.wait_ge(toeplitz_loaded, 16 * T * (q + 1))
                    for b in range(JB):
                        o = y_ps[:, g % 2, b * P:(b + 1) * P]
                        pe.matmul(o, u_t[:, g, b * P:(b + 1) * P], toeplitz[:, g], start=True, stop=False)
                        for d in range(2):
                            i = 2 * g + d
                            cols = slice(b * P + d, (b + 1) * P + d)
                            for k, c in enumerate((cp, cp_swap)):
                                first = 0 if d else 1
                                last = pe.matmul(o, x_st[:, x_slot(i), k, cols],
                                                 c[:, pair(i), first:first + T].rearrange("p s h -> p (s h)"),
                                                 start=False, stop=(d == 1 and k == 1))
                    last.then_inc(y_done, 1)

                for i in range(PAIRS):
                    inputs(i)
                    if i >= 6 and i % 2 == 0:
                        outputs((i - 6) // 2)
                for g in range(G - 3, G):
                    outputs(g)

            def body(q):
                pe.wait_ge(ug_ready, q + 1)
                ug = uz[:].rearrange("p b (g c) -> p b g c", g=G)
                for t in range(U_TURNS):
                    turn(q, t, [ug[:, b, g] for g in (2 * t, 2 * t + 1) for b in range(JB)])
                pe.wait_ge(bp_ready, q + 1)
                for t in range(B_TURNS):
                    turn(q, U_TURNS + t, [bp[:, p].rearrange("p s h -> p (s h)") for p in range(4 * t, 4 * t + 4)])
                pe.wait_ge(cp_ready, q + 1)
                lags(q, 0)
                lags(q, 1)
                pe.wait_ge(turn_out, q * QT + U_TURNS + B_TURNS)
                if static(q):
                    pe.wait_ge(edges_ready, XR)
                main(q)
                pe.wait_ge(z_ready, q * G + G)
                for t in range(Z_TURNS):
                    b, s4 = t // 2, t % 2
                    turn(q, U_TURNS + B_TURNS + t, [first_chunk[:, b, s] for s in range(4 * s4, 4 * s4 + 4)])

            pe.wait_ge(const_step, 8)
            pe.wait_ge(const_loaded, 64)
            quarters(pe, body)
            pe.wait_ge(turn_out, NQU * QT)
            for n in range(4 * NTB):
                tb, c = n // 4, n % 4
                wait(pe, gate_ready, n - 1)
                for k in range(4):
                    last = pe.matmul(y_ps[:, n % 2], wg[:, k, c * P:(c + 1) * P], z_t[:, k, tb * TB:(tb + 1) * TB],
                                     start=(k == 0), stop=(k == 3))
                last.then_inc(glu_done, 1)


def phase_mlp(nc, x_t, att_s, total_s, ssm_s, w_stream, gains, y_t):
    PIECE = 1024
    RAW = 4
    TURNS = 18
    OUT_TURNS, UP_TURNS, DOWN_TURNS = 2, 4, 2
    HALF_TURNS = UP_TURNS + 2 * DOWN_TURNS
    MIX_ORDER = list(range(H, KD)) + list(range(H))
    LAM_INIT = 0.8 - 0.6 * math.exp(0.0)
    with ExitStack() as ctx:
        m = Memory(nc, ctx, "ml")
        w_raw = m.sb("w_raw", [P, RAW, PIECE])
        w_hi = m.sb("w_hi", [P, 2, PIECE], F32R)
        w_lo = m.sb("w_lo", [P, 2, PIECE], F32R)
        act_hi = m.sb("act_hi", [P, 16, TB], F32R)
        act_lo = m.sb("act_lo", [P, 16, TB], F32R)
        hg_hi = m.sb("hg_hi", [P, KD, TB], F32R)
        hg_lo = m.sb("hg_lo", [P, KD, TB], F32R)
        h = m.sb("h", [P, KD, TB])
        x_acc = m.sb("x_acc", [P, KD, TB])
        mix = m.sb("mix", [P, KD, TB])
        rms_att = m.sb("rms_att", [P, H, TB])
        relu = m.sb("relu", [P, 2, TB])
        relu_sq = m.sb("relu_sq", [P, 2, TB])
        square = m.sb("square", [P, TB])
        sums = m.sb("sums", [P, TB])
        sums2 = m.sb("sums2", [P, TB])
        inv_var = m.sb("inv_var", [P, TB])
        rms_y = m.sb("rms_y", [P, TB])
        y = m.sb("y", [P, 2, TB])
        gain = m.sb("gain", [P, 2 * KD + 1])
        gain_att = m.sb("gain_att", [P, 1])
        ones = m.sb("ones", [P, P])
        eps_c = m.sb("eps_c", [P, 1])
        work = m.ps("work", [P, 2, TB])
        down = m.ps("down", [P, 4, TB])
        stat = m.ps("stat", [P, TB])

        consts_ready = m.sem("consts_ready")
        gain_loaded = m.sem("gain_loaded")
        gain_att_ready = m.sem("gain_att_ready")
        waited = m.sem("waited")
        raw_loaded = [m.sem(f"raw_loaded{i}") for i in range(RAW)]
        w_hi_ready = m.sem("w_hi_ready")
        w_lo_ready = m.sem("w_lo_ready")
        piece_done = m.sem("piece_done")
        inputs_loaded = m.sem("inputs_loaded")
        x_loaded = m.sem("x_loaded")
        rms_att_ready = m.sem("rms_att_ready")
        inv_att_ready = m.sem("inv_att_ready")
        mix_ready = m.sem("mix_ready")
        mix_hi_ready = m.sem("mix_hi_ready")
        mix_lo_ready = m.sem("mix_lo_ready")
        h_ready = m.sem("h_ready")
        hg_hi_ready = m.sem("hg_hi_ready")
        hg_lo_ready = m.sem("hg_lo_ready")
        sum_step = m.sem("sum_step")
        sums_ready = m.sem("sums_ready")
        stat_done = m.sem("stat_done")
        inv_step = m.sem("inv_step")
        relu_ready = m.sem("relu_ready")
        relu_sq_ready = m.sem("relu_sq_ready")
        act_hi_ready = m.sem("act_hi_ready")
        act_lo_ready = m.sem("act_lo_ready")
        down_done = m.sem("down_done")
        down_free = m.sem("down_free")
        down_step = m.sem("down_step")
        sum2_step = m.sem("sum2_step")
        sums2_ready = m.sem("sums2_ready")
        stat2_done = m.sem("stat2_done")
        rms_y_ready = m.sem("rms_y_ready")
        inv_y_ready = m.sem("inv_y_ready")
        y_ready = m.sem("y_ready")
        y_stored = [m.sem("y_stored0"), m.sem("y_stored1")]
        block = ctx.enter_context(nc.Block())

        def static(x):
            return isinstance(x, int)

        @block.sync
        def _(sp):
            def load(p, q, r):
                if not static(p) or p >= RAW:
                    sp.wait_ge(w_lo_ready, p - RAW + 1)
                sp.dma_start(w_raw[:, r], w_stream[bass.ds(q, 1)].rearrange("o p n -> (o p) n")).then_inc(raw_loaded[r], 16)

            sp.dma_start(gain[:], gains).then_inc(gain_loaded, 16)
            for r in range(RAW):
                load(r, r, r)

            def body(tb, ahead):
                with sp.Fori(1, TURNS) as turn:
                    for r in range(RAW):
                        load((tb * TURNS + turn) * RAW + r, turn * RAW + r, r)
                for r in range(ahead):
                    load((tb + 1) * (TURNS * RAW) + r, r, r)

            with sp.Fori(0, NTB - 1) as tb:
                body(tb, RAW)
            body(NTB - 1, 2)

        @block.gpsimd
        def _(pool):
            pool.memset(ones[:], 1.0).then_inc(consts_ready, 1)
            pool.memset(eps_c[:], EPS).then_inc(consts_ready, 1)
            pool.sem_inc(relu_sq_ready, 2)
            pool.sem_inc(down_free, 4)

            def wait(sem, value):
                pool.wait_ge(sem, value)
                pool.sem_inc(waited, 1)

            def load_inputs(tb):
                t = bass.ds(tb * TB, TB)
                if not static(tb) or tb > 0:
                    wait(mix_lo_ready, tb * KD)
                pool.dma_start(mix[:, 0:H], att_s.rearrange("h p t -> p h t")[:, :, t]).then_inc(inputs_loaded, 16)
                pool.dma_start(rms_att[:], total_s.rearrange("h p t -> p h t")[:, :, t]).then_inc(inputs_loaded, 16)
                pool.dma_start(mix[:, H:KD], ssm_s.rearrange("h p t -> p h t")[:, :, t]).then_inc(inputs_loaded, 16)

            def load_x(tb):
                if not static(tb) or tb > 0:
                    wait(sums2_ready, tb)
                pool.dma_start(x_acc[:], x_t.rearrange("(k p) t -> p k t", p=P)[:, :, bass.ds(tb * TB, TB)])\
                    .then_inc(x_loaded, 16)

            def store_y(tb):
                for k in range(KD):
                    wait(y_ready, tb * KD + k + 1)
                    pool.dma_start(y_t[k * P:(k + 1) * P, bass.ds(tb * TB, TB)], y[:, k % 2]).then_inc(y_stored[k % 2], 16)

            load_inputs(0)
            load_x(0)
            with pool.Fori(0, NTB - 1) as tb:
                load_inputs(tb + 1)
                load_x(tb + 1)
                store_y(tb)
            store_y(NTB - 1)
            for i in range(2):
                pool.wait_ge(y_stored[i], 16 * NTB * KD // 2)

        def split_high(act, turn, r):
            act.wait_ge(piece_done, turn * RAW + r + 1)
            act.wait_ge(raw_loaded[(r + 2) % RAW], (turn + (r + 2) // RAW + 1) * 16)
            act.activation(w_hi[:, r % 2], w_raw[:, (r + 2) % RAW], ACT.Copy).then_inc(w_hi_ready, 1)

        def split_low(dve, turn, r):
            dve.wait_ge(w_hi_ready, turn * RAW + r + 3)
            dve.tensor_tensor(w_lo[:, r % 2], w_raw[:, (r + 2) % RAW], w_hi[:, r % 2].bitcast(F32), ALU.subtract)\
                .then_inc(w_lo_ready, 1)

        def segments(eng, tb, out, up, down_piece, down_end):
            start = tb * TURNS
            for ct in range(OUT_TURNS * RAW):
                out(start + ct // RAW, ct % RAW, ct)
            for half in range(2):
                at = start + OUT_TURNS + half * HALF_TURNS
                with eng.Fori(0, UP_TURNS) as t:
                    for r in range(RAW):
                        up(at + t, r, t * RAW + r, half)
                for wide in range(2):
                    for piece in range(DOWN_TURNS * RAW):
                        down_piece(at + UP_TURNS + wide * DOWN_TURNS + piece // RAW, piece % RAW, piece)
                    down_end(half, wide)

        @block.scalar
        def _(act):
            def mix_rms(tb):
                act.wait_ge(inputs_loaded, tb * 48 + 48)
                act.activation(rms_att[:], rms_att[:], ACT.Sqrt, scale=1.0 / P).then_inc(rms_att_ready, 1)

            def mix_high(tb):
                for k in MIX_ORDER:
                    if k == 0:
                        act.wait_ge(mix_ready, tb + 1)
                    act.activation(act_hi[:, k], mix[:, k], ACT.Copy).then_inc(mix_hi_ready, 1)

            def body(tb, last):
                def out(turn, r, ct):
                    split_high(act, turn, r)
                    act.wait_ge(h_ready, tb * KD + ct + 1)
                    act.activation(hg_hi[:, ct], h[:, ct], ACT.Copy, scale=gain[:, ct:ct + 1]).then_inc(hg_hi_ready, 1)

                def up(turn, r, ff, half):
                    split_high(act, turn, r)
                    n = tb * 32 + half * 16 + ff
                    act.wait_ge(relu_sq_ready, n + 1)
                    act.activation(relu[:, r % 2], work[:, r % 2], ACT.Relu).then_inc(relu_ready, 1)
                    act.wait_ge(relu_ready, n + 1)
                    act.activation(act_hi[:, bass.ds(ff, 1)], relu[:, r % 2:r % 2 + 1], ACT.Square).then_inc(act_hi_ready, 1)

                def down_piece(turn, r, piece):
                    split_high(act, turn, r)

                def down_end(half, wide):
                    if half:
                        return
                    for c in range(4):
                        if c < 3:
                            act.wait_ge(down_done, (tb * 4 + wide) * 3 + c + 1)
                        act.activation(x_acc[:, 4 * wide + c], down[:, c], ACT.Copy).then_inc(down_free, 1)
                    if wide and not last:
                        mix_rms(tb + 1)

                segments(act, tb, out, up, down_piece, down_end)
                if not last:
                    mix_high(tb + 1)
                act.wait_ge(stat2_done, tb + 1)
                act.activation(rms_y[:], stat[:], ACT.Sqrt, bias=eps_c[:], scale=1.0 / D).then_inc(rms_y_ready, 1)

            act.wait_ge(gain_loaded, 16)
            act.wait_ge(consts_ready, 2)
            for r in range(2):
                act.wait_ge(raw_loaded[r], 16)
                act.activation(w_hi[:, r], w_raw[:, r], ACT.Copy).then_inc(w_hi_ready, 1)
            mix_rms(0)
            mix_high(0)
            with act.Fori(0, NTB - 1) as tb:
                body(tb, False)
            body(NTB - 1, True)

        @block.vector
        def _(dve):
            def mix_scale(tb):
                dve.wait_ge(rms_att_ready, tb + 1)
                dve.reciprocal(rms_att[:], rms_att[:]).then_inc(inv_att_ready, 1)
                dve.wait_ge(inv_att_ready, tb + 1)
                dve.scalar_tensor_tensor(mix[:, 0:H], mix[:, 0:H], gain_att[:, 0:1], rms_att[:], ALU.mult, ALU.mult)\
                    .then_inc(mix_ready, 1)

            def mix_low(tb):
                for i, k in enumerate(MIX_ORDER):
                    dve.wait_ge(mix_hi_ready, tb * KD + i + 1)
                    dve.tensor_tensor(act_lo[:, k], mix[:, k], act_hi[:, k].bitcast(F32), ALU.subtract)\
                        .then_inc(mix_lo_ready, 1)

            def add_square(k, total, step, base, ready):
                if k == 0:
                    dve.tensor_tensor(total[:], h[:, k], h[:, k], ALU.mult).then_inc(step, 1)
                    return
                dve.tensor_tensor(square[:], h[:, k], h[:, k], ALU.mult).then_inc(step, 1)
                dve.wait_ge(step, base + 2 * k)
                dve.tensor_tensor(total[:], total[:], square[:], ALU.add).then_inc(step if k < KD - 1 else ready, 1)

            def body(tb, last):
                def out(turn, r, ct):
                    split_low(dve, turn, r)
                    if ct == 0:
                        dve.wait_ge(x_loaded, tb * 16 + 16)
                    dve.tensor_tensor(h[:, ct], work[:, ct % 2], x_acc[:, ct], ALU.add).then_inc(h_ready, 1)
                    dve.wait_ge(h_ready, tb * KD + ct + 1)
                    add_square(ct, sums, sum_step, tb * (2 * KD - 2), sums_ready)
                    dve.wait_ge(hg_hi_ready, tb * KD + ct + 1)
                    dve.scalar_tensor_tensor(hg_lo[:, ct], h[:, ct], gain[:, ct:ct + 1], hg_hi[:, ct].bitcast(F32),
                                             ALU.mult, ALU.subtract).then_inc(hg_lo_ready, 1)

                def up(turn, r, ff, half):
                    split_low(dve, turn, r)
                    n = tb * 32 + half * 16 + ff
                    dve.wait_ge(relu_ready, n + 1)
                    dve.tensor_tensor(relu_sq[:, r % 2], relu[:, r % 2], work[:, r % 2], ALU.mult).then_inc(relu_sq_ready, 1)
                    dve.wait_ge(act_hi_ready, n + 1)
                    dve.wait_ge(relu_sq_ready, n + 3)
                    dve.tensor_tensor(act_lo[:, bass.ds(ff, 1)], relu_sq[:, r % 2:r % 2 + 1],
                                      act_hi[:, bass.ds(ff, 1)].bitcast(F32), ALU.subtract).then_inc(act_lo_ready, 1)

                def down_piece(turn, r, piece):
                    split_low(dve, turn, r)

                def down_end(half, wide):
                    if half == 0:
                        if wide:
                            dve.wait_ge(stat_done, tb + 1)
                            dve.tensor_scalar(inv_var[:], stat[:], 1.0 / D, EPS, ALU.mult, ALU.add).then_inc(inv_step, 1)
                            dve.wait_ge(inv_step, tb * 2 + 1)
                            dve.reciprocal(inv_var[:], inv_var[:]).then_inc(inv_step, 1)
                            dve.wait_ge(inv_step, tb * 2 + 2)
                            if not last:
                                mix_scale(tb + 1)
                        return
                    if wide == 0:
                        dve.wait_ge(down_free, 4 + tb * 16 + 8)
                    for c in range(4):
                        ct = 4 * wide + c
                        if c < 3:
                            dve.wait_ge(down_done, (tb * 4 + 2 + wide) * 3 + c + 1)
                        dve.tensor_tensor(x_acc[:, ct], down[:, c], x_acc[:, ct], ALU.add).then_inc(down_free, 1)
                        dve.wait_ge(down_free, 4 + tb * 16 + 8 + ct + 1)
                        dve.tensor_tensor(x_acc[:, ct], x_acc[:, ct], inv_var[:], ALU.mult).then_inc(down_step, 1)
                        dve.wait_ge(down_step, (tb * KD + ct) * 2 + 1)
                        dve.tensor_tensor(h[:, ct], x_acc[:, ct], h[:, ct], ALU.add).then_inc(down_step, 1)
                        dve.wait_ge(down_step, (tb * KD + ct) * 2 + 2)
                        add_square(ct, sums2, sum2_step, tb * (2 * KD - 2), sums2_ready)

                segments(dve, tb, out, up, down_piece, down_end)
                if not last:
                    mix_low(tb + 1)
                dve.wait_ge(rms_y_ready, tb + 1)
                dve.reciprocal(rms_y[:], rms_y[:]).then_inc(inv_y_ready, 1)
                dve.wait_ge(inv_y_ready, tb + 1)
                for k in range(KD):
                    if k >= 2:
                        dve.wait_ge(y_stored[k % 2], 16 * (tb * (KD // 2) + k // 2))
                    elif not static(tb) or tb > 0:
                        dve.wait_ge(y_stored[k % 2], 16 * (tb * (KD // 2)))
                    dve.scalar_tensor_tensor(y[:, k % 2], h[:, k], gain[:, KD + k:KD + k + 1], rms_y[:],
                                             ALU.mult, ALU.mult).then_inc(y_ready, 1)

            dve.wait_ge(gain_loaded, 16)
            dve.tensor_scalar(gain_att[:], gain[:, 2 * KD:2 * KD + 1], 1.0 - LAM_INIT, None, ALU.mult)\
                .then_inc(gain_att_ready, 1)
            dve.wait_ge(gain_att_ready, 1)
            for r in range(2):
                dve.wait_ge(w_hi_ready, r + 1)
                dve.tensor_tensor(w_lo[:, r], w_raw[:, r], w_hi[:, r].bitcast(F32), ALU.subtract).then_inc(w_lo_ready, 1)
            mix_scale(0)
            mix_low(0)
            body(0, False)
            with dve.Fori(1, NTB - 1) as tb:
                body(tb, False)
            body(NTB - 1, True)

        @block.tensor
        def _(pe):
            def statistics(total, ready, done, tb):
                pe.wait_ge(ready, tb + 1)
                pe.matmul(stat[:], ones[:], total[:], start=True, stop=True).then_inc(done, 1)

            def product(out, lhs_hi, lhs_lo, rhs_hi, rhs_lo, first, last):
                pe.matmul(out, lhs_hi, rhs_hi, start=first, stop=False)
                pe.matmul(out, lhs_hi, rhs_lo, start=False, stop=False)
                return pe.matmul(out, lhs_lo, rhs_hi, start=False, stop=last)

            def body(tb):
                def out(turn, r, ct):
                    pe.wait_ge(w_lo_ready, turn * RAW + r + 1)
                    if ct >= 2:
                        pe.wait_ge(h_ready, tb * KD + ct - 1)
                    for i, k in enumerate(MIX_ORDER):
                        if ct == 0:
                            pe.wait_ge(mix_lo_ready, tb * KD + i + 1)
                        w = slice(k * P, (k + 1) * P)
                        last = product(work[:, ct % 2], w_hi[:, r % 2, w], w_lo[:, r % 2, w], act_hi[:, k], act_lo[:, k],
                                       i == 0, i == KD - 1)
                    last.then_inc(piece_done, 1)
                    if ct == 0 and not (static(tb) and tb == 0):
                        statistics(sums2, sums2_ready, stat2_done, tb - 1)

                def up(turn, r, ff, half):
                    pe.wait_ge(w_lo_ready, turn * RAW + r + 1)
                    pe.wait_ge(relu_sq_ready, tb * 32 + half * 16 + ff + 1)
                    pe.wait_ge(hg_lo_ready, (tb + 1) * KD)
                    for k in range(KD):
                        w = slice(k * P, (k + 1) * P)
                        last = product(work[:, r % 2], w_hi[:, r % 2, w], w_lo[:, r % 2, w], hg_hi[:, k], hg_lo[:, k],
                                       k == 0, k == KD - 1)
                    last.then_inc(piece_done, 1)

                start = tb * TURNS
                for ct in range(OUT_TURNS * RAW):
                    out(start + ct // RAW, ct % RAW, ct)
                statistics(sums, sums_ready, stat_done, tb)
                with pe.Fori(0, 2) as half:
                    at = start + OUT_TURNS + half * HALF_TURNS
                    with pe.Fori(0, UP_TURNS) as t:
                        for r in range(RAW):
                            up(at + t, r, t * RAW + r, half)
                    with pe.Fori(0, 2) as wide:
                        seg = tb * 4 + half * 2 + wide
                        for piece in range(DOWN_TURNS * RAW):
                            turn, r = at + UP_TURNS + wide * DOWN_TURNS + piece // RAW, piece % RAW
                            final = piece == DOWN_TURNS * RAW - 1
                            pe.wait_ge(w_lo_ready, turn * RAW + r + 1)
                            pe.wait_ge(act_lo_ready, tb * 32 + half * 16 + 2 * piece + 2)
                            for c in range(4):
                                if piece == 0:
                                    pe.wait_ge(down_free, seg * 4 + c + 1)
                                for i in range(2):
                                    w = slice(i * (4 * P) + c * P, i * (4 * P) + (c + 1) * P)
                                    last = product(down[:, c], w_hi[:, r % 2, w], w_lo[:, r % 2, w],
                                                   act_hi[:, 2 * piece + i], act_lo[:, 2 * piece + i],
                                                   piece == 0 and i == 0, final and i == 1)
                                if final and c < 3:
                                    last.then_inc(down_done, 1)
                            last.then_inc(piece_done, 1)

            pe.wait_ge(consts_ready, 2)
            body(0)
            with pe.Fori(1, NTB) as tb:
                body(tb)
            statistics(sums2, sums2_ready, stat2_done, NTB - 1)


def weight_stream(w_out, w1, w2):
    def columns(w):
        k, n = w.shape
        return w.reshape(k // P, P, n // P, P).transpose(2, 1, 0, 3).reshape(n // P, P, k)

    def rows(w):
        return w.reshape(2, 8, 2, P, 2, D // 2).transpose(0, 4, 1, 3, 2, 5).reshape(2, 16, P, D)

    up, down = columns(w1).reshape(2, 16, P, D), rows(w2)
    return np.ascontiguousarray(np.concatenate([columns(w_out), up[0], down[0], up[1], down[1]]))


def ssm_layout(inputs):
    def pairs(a):
        a = np.asarray(a)
        return a.reshape(2, 4, 8, *a.shape[2:]).swapaxes(0, 1).reshape(64, *a.shape[2:])

    def both(a, b):
        return np.concatenate([a.swapaxes(0, 1), b.swapaxes(0, 1)])

    re, im = pairs(inputs["ssm_lam_re"][0]), pairs(inputs["ssm_lam_im"][0])
    log_dt = np.broadcast_to(pairs(inputs["ssm_log_dt"][0])[:, None], re.shape)
    par = np.stack([both(a, a) for a in (re, im, log_dt)], axis=1)
    b_re, b_im = pairs(inputs["ssm_b_re"][0]), pairs(inputs["ssm_b_im"][0])
    c_re, c_im = (pairs(inputs[n][0]).swapaxes(1, 2) for n in ("ssm_c_re", "ssm_c_im"))
    bc = np.stack([both(b_re, b_im), both(b_im, b_re), both(c_re, c_im), both(c_im, c_re)], axis=1)
    bc = bc.reshape(P, 4, 4, 16, 16).transpose(2, 0, 1, 3, 4)
    skip = np.asarray(inputs["ssm_d"][0]).reshape(32, 16).T
    w_glu = np.asarray(inputs["w_glu"][0]).reshape(4, P, ATT).transpose(1, 0, 2)
    b_glu = np.asarray(inputs["b_glu"][0]).reshape(4, P).T
    return [np.ascontiguousarray(a) for a in (par, skip, bc, w_glu, b_glu)]


def encoder_block(nc, x_t, norm1_g, w_in, lam_in, s_par, s_d, s_bc, w_glu, b_glu, w_stream, gains, y_t):
    def scratch(name, shape):
        return nc.dram_tensor(name, shape, F32, kind="Internal").ap()

    qk_s = scratch("qk_s", [NQK, P, S])
    v_s = scratch("v_s", [S, ATT])
    u_s = scratch("u_s", [S, ATT])
    att_s = scratch("att_s", [H, P, S])
    total_s = scratch("total_s", [H, P, S])
    ssm_s = scratch("ssm_s", [ATT // P, P, S])
    phase_project(nc, x_t, norm1_g, w_in, qk_s, v_s, u_s)
    phase_ssm(nc, s_par, s_d, s_bc, w_glu, b_glu, u_s, ssm_s)
    phase_attention(nc, lam_in, qk_s, v_s, att_s, total_s)
    phase_mlp(nc, x_t, att_s, total_s, ssm_s, w_stream, gains, y_t)


def kernel(**inputs):
    import concourse.bacc as _bacc
    from concourse.bass_utils import run_bass_kernel_spmd as _run

    a = {k: np.asarray(v) for k, v in inputs.items()}

    def per_tile(v):
        return v.reshape(-1, P).T

    lam = np.stack([a[n][0] for n in ("lam_q1", "lam_k1", "lam_q2", "lam_k2")])
    gains = np.concatenate([per_tile(a["norm2_g"][0]), per_tile(a["final_g"]), per_tile(a["subln_g"][0])], axis=1)
    s_par, s_d, s_bc, w_glu, b_glu = ssm_layout(a)
    laid_out = {
        "x_t": a["x"][0].T, "norm1_g": per_tile(a["norm1_g"][0]), "w_in": a["w_in"][0],
        "lam": np.broadcast_to(lam, (P, *lam.shape)), "s_par": s_par, "s_d": s_d, "s_bc": s_bc,
        "w_glu": w_glu, "b_glu": b_glu,
        "w_stream": weight_stream(a["w_out"][0], a["w_mlp1"][0], a["w_mlp2"][0]), "gains": gains}
    nc = _bacc.Bacc("TRN2", target_bir_lowering=False, num_devices=1)
    arrays, args = {}, []
    for name, v in laid_out.items():
        arrays[f"in_{name}"] = v = np.ascontiguousarray(v)
        args.append(nc.dram_tensor(f"in_{name}", v.shape, F32, kind="ExternalInput").ap())
    args.append(nc.dram_tensor("y_t", (D, S), F32, kind="ExternalOutput").ap())
    encoder_block(nc, *args)
    r = _run(nc, [arrays], core_ids=[0])
    return np.ascontiguousarray(r.results[0]["y_t"].T)[None]
```

```python
import math
from contextlib import ExitStack

import numpy as np

import concourse.bass as bass
from concourse import mybir

F32 = mybir.dt.float32
F32R = mybir.dt.float32r
F16 = mybir.dt.float16
I32 = mybir.dt.int32
ALU = mybir.AluOpType
ACT = mybir.ActivationFunctionType
AX_X = mybir.AxisListType.X

P = 128
D = 1024
S = 2048
TB = 512
NTB = S // TB
KD = D // P
ATT = 512
H = 4
DH = 64
EPS = 1e-6
IN_W = 3 * ATT + ATT
NQK = 2 * ATT // P


class Memory:

    def __init__(self, nc, ctx, tag):
        self.nc, self.ctx, self.tag = nc, ctx, tag

    def sb(self, name, shape, dt=F32):
        return self.ctx.enter_context(self.nc.sbuf_tensor(f"{self.tag}_{name}", shape, dt))

    def ps(self, name, shape, dt=F32):
        return self.ctx.enter_context(self.nc.psum_tensor(f"{self.tag}_{name}", shape, dt))

    def sem(self, name):
        return self.ctx.enter_context(self.nc.semaphore(f"{self.tag}_{name}"))


def phase_project(nc, x_t, norm1_g, w_in, qk_s, v_s, u_s):
    BANKS = 6
    GROUPS = NQK + 2 * (TB // P)
    NPIECE = IN_W // P
    EARLY = 7
    with ExitStack() as ctx:
        m = Memory(nc, ctx, "pj")
        w_raw = m.sb("w_raw", [P, 2, KD, P])
        w_hi = m.sb("w_hi", [P, KD, IN_W], F32R)
        w_lo = m.sb("w_lo", [P, KD, IN_W], F32R)
        x_raw = m.sb("x_raw", [P, KD, TB])
        x_hi = m.sb("x_hi", [P, KD, TB], F32R)
        x_lo = m.sb("x_lo", [P, KD, TB], F32R)
        square = m.sb("square", [P, TB])
        square_sum = m.sb("square_sum", [P, TB])
        rms_b = m.sb("rms_b", [P, TB])
        rinv_b = m.sb("rinv_b", [P, TB])
        rms_t = m.sb("rms_t", [P, TB // P])
        rinv_t = m.sb("rinv_t", [P, TB // P])
        gain = m.sb("gain", [P, KD])
        ones = m.sb("ones", [P, P])
        eps_c = m.sb("eps_c", [P, 1])
        qk_out = m.sb("qk_out", [P, 2, TB])
        vu_out = m.sb("vu_out", [P, 2, ATT])
        acc = m.ps("acc", [P, BANKS, TB])
        stat_b = m.ps("stat_b", [P, TB])
        stat_t = m.ps("stat_t", [P, TB])

        gain_loaded = m.sem("gain_loaded")
        consts_ready = m.sem("consts_ready")
        x_loaded = [m.sem("x_loaded0"), m.sem("x_loaded1")]
        w_loaded = [m.sem("w_loaded0"), m.sem("w_loaded1")]
        w_hi_ready = m.sem("w_hi_ready")
        w_lo_ready = m.sem("w_lo_ready")
        x_hi_ready = m.sem("x_hi_ready")
        x_lo_ready = m.sem("x_lo_ready")
        pool_step = m.sem("pool_step")
        squares_ready = m.sem("squares_ready")
        stats_done = m.sem("stats_done")
        rms_ready = m.sem("rms_ready")
        rinv_ready = m.sem("rinv_ready")
        group_done = m.sem("group_done")
        qk_evacuated = m.sem("qk_evacuated")
        vu_evacuated = m.sem("vu_evacuated")
        qk_stored = [m.sem("qk_stored0"), m.sem("qk_stored1")]
        vu_stored = [m.sem("vu_stored0"), m.sem("vu_stored1")]
        block = ctx.enter_context(nc.Block())
        w_pieces = w_in.rearrange("(k p) n -> p k n", p=P)
        x_tiles = x_t.rearrange("(k p) t -> p k t", p=P)

        def evacuated_before(eng, tb, g):
            prev, back = (g - BANKS, tb) if g >= BANKS else (
                max(x for x in range(GROUPS) if x % BANKS == g % BANKS), tb - 1)
            if isinstance(back, int) and back < 0:
                return
            if prev < NQK:
                eng.wait_ge(qk_evacuated, back * NQK + prev + 1)
            else:
                eng.wait_ge(vu_evacuated, back * (GROUPS - NQK) + prev - NQK + 1)

        @block.sync
        def _(sp):
            sp.dma_start(gain[:], norm1_g).then_inc(gain_loaded, 16)

            def load_w(i):
                if i >= 2:
                    sp.wait_ge(w_lo_ready, i - 1)
                sp.dma_start(w_raw[:, i % 2], w_pieces[:, :, i * P:(i + 1) * P]).then_inc(w_loaded[i % 2], 16)

            def stores(tb, gs):
                for g in gs:
                    if g < NQK:
                        sp.wait_ge(qk_evacuated, tb * NQK + g + 1)
                        sp.dma_start(qk_s[g, :, bass.ds(tb * TB, TB)], qk_out[:, g % 2]).then_inc(qk_stored[g % 2], 16)
                    else:
                        e = g - NQK
                        sp.wait_ge(vu_evacuated, tb * (GROUPS - NQK) + e + 1)
                        dst = v_s if e % 2 == 0 else u_s
                        sp.dma_start(dst[bass.ds(tb * TB + (e // 2) * P, P), :], vu_out[:, e % 2])\
                            .then_inc(vu_stored[e % 2], 16)

            def load_half_x(tb, i):
                ks = slice(i * KD // 2, (i + 1) * KD // 2)
                sp.dma_start(x_raw[:, ks], x_tiles[:, ks, bass.ds(tb * TB, TB)]).then_inc(x_loaded[i], 16)

            def load_x(tb):
                if not isinstance(tb, int) or tb > 0:
                    sp.wait_ge(x_hi_ready, tb * KD)
                    sp.wait_ge(x_lo_ready, tb * KD)
                    sp.wait_ge(squares_ready, tb)
                for i in range(2):
                    load_half_x(tb, i)

            load_half_x(0, 0)
            load_w(0)
            load_half_x(0, 1)
            stored = 0
            for i in range(1, NPIECE):
                if i >= EARLY + 2 and (i - EARLY - 2) % 3 == 0:
                    stores(0, [stored])
                    stored += 1
                load_w(i)
            stores(0, range(stored, GROUPS // 2))
            with sp.Fori(1, NTB) as tb:
                load_x(tb)
                stores(tb - 1, range(GROUPS // 2, GROUPS))
                stores(tb, range(GROUPS // 2))
            stores(NTB - 1, range(GROUPS // 2, GROUPS))
            for s in range(2):
                sp.wait_ge(qk_stored[s], 16 * NTB * NQK // 2)
                sp.wait_ge(vu_stored[s], 16 * NTB * (GROUPS - NQK) // 2)

        @block.gpsimd
        def _(pool):
            pool.memset(ones[:], 1.0).then_inc(consts_ready, 1)
            pool.memset(eps_c[:], EPS).then_inc(consts_ready, 1)

            with pool.Fori(0, NTB) as tb:
                pool.wait_ge(x_loaded[0], tb * 16 + 16)
                steps = 2 * KD - 2
                pool.tensor_tensor(square_sum[:], x_raw[:, 0], x_raw[:, 0], ALU.mult).then_inc(pool_step, 1)
                for k in range(1, KD):
                    if k == KD // 2:
                        pool.wait_ge(x_loaded[1], tb * 16 + 16)
                    pool.wait_ge(pool_step, tb * steps + 2 * k - 1)
                    pool.tensor_tensor(square[:], x_raw[:, k], x_raw[:, k], ALU.mult).then_inc(pool_step, 1)
                    pool.wait_ge(pool_step, tb * steps + 2 * k)
                    pool.tensor_tensor(square_sum[:], square_sum[:], square[:], ALU.add)\
                        .then_inc(pool_step if k < KD - 1 else squares_ready, 1)
                pool.wait_ge(stats_done, tb + 1)

        @block.scalar
        def _(act):
            def split_w(i):
                act.wait_ge(w_loaded[i % 2], 16 * (i // 2 + 1))
                act.activation(w_hi[:, :, i * P:(i + 1) * P], w_raw[:, i % 2], ACT.Copy).then_inc(w_hi_ready, 1)

            def split_x(tb):
                if not isinstance(tb, int) or tb > 0:
                    act.wait_ge(group_done, tb * GROUPS)
                for k in range(KD):
                    if k % (KD // 2) == 0:
                        act.wait_ge(x_loaded[k // (KD // 2)], tb * 16 + 16)
                    act.activation(x_hi[:, k], x_raw[:, k], ACT.Copy, scale=gain[:, k:k + 1]).then_inc(x_hi_ready, 1)

            def stats(tb):
                act.wait_ge(stats_done, tb + 1)
                if not isinstance(tb, int) or tb > 0:
                    act.wait_ge(rinv_ready, tb)
                act.activation(rms_b[:], stat_b[:], ACT.Sqrt, bias=eps_c[:], scale=1.0 / D)
                act.activation(rms_t[:], stat_t[:, 0:TB // P], ACT.Sqrt, bias=eps_c[:], scale=1.0 / D)\
                    .then_inc(rms_ready, 1)

            def evacuate_vu(tb, e):
                act.wait_ge(group_done, tb * GROUPS + NQK + e + 1)
                if e < 2:
                    if not isinstance(tb, int) or tb > 0:
                        act.wait_ge(vu_stored[e % 2], tb * 16 * ((GROUPS - NQK) // 2))
                else:
                    act.wait_ge(vu_stored[e % 2], tb * 16 * ((GROUPS - NQK) // 2) + 16 * (e // 2))
                act.activation(vu_out[:, e % 2], acc[:, (NQK + e) % BANKS], ACT.Copy,
                               scale=rinv_t[:, e // 2:e // 2 + 1]).then_inc(vu_evacuated, 1)

            act.wait_ge(gain_loaded, 16)
            act.wait_ge(consts_ready, 2)
            split_x(0)
            for i in range(NPIECE):
                if i == EARLY:
                    stats(0)
                split_w(i)
            act.wait_ge(rinv_ready, 1)
            for e in range(GROUPS - NQK):
                evacuate_vu(0, e)
            with act.Fori(1, NTB) as tb:
                split_x(tb)
                stats(tb)
                act.wait_ge(rinv_ready, tb + 1)
                for e in range(GROUPS - NQK):
                    evacuate_vu(tb, e)

        @block.vector
        def _(dve):
            def split_w(i):
                dve.wait_ge(w_hi_ready, i + 1)
                dve.tensor_tensor(w_lo[:, :, i * P:(i + 1) * P], w_raw[:, i % 2],
                                  w_hi[:, :, i * P:(i + 1) * P].bitcast(F32), ALU.subtract).then_inc(w_lo_ready, 1)

            def split_x(tb):
                for k in range(KD):
                    dve.wait_ge(x_hi_ready, tb * KD + k + 1)
                    dve.scalar_tensor_tensor(x_lo[:, k], x_raw[:, k], gain[:, k:k + 1], x_hi[:, k].bitcast(F32),
                                             ALU.mult, ALU.subtract).then_inc(x_lo_ready, 1)

            def invert(tb):
                dve.wait_ge(rms_ready, tb + 1)
                if not isinstance(tb, int) or tb > 0:
                    dve.wait_ge(vu_evacuated, tb * (GROUPS - NQK))
                dve.reciprocal(rinv_b[:], rms_b[:])
                dve.reciprocal(rinv_t[:], rms_t[:]).then_inc(rinv_ready, 1)
                dve.wait_ge(rinv_ready, tb + 1)

            def evacuate_qk(tb, g):
                dve.wait_ge(group_done, tb * GROUPS + g + 1)
                if g < 2:
                    if not isinstance(tb, int) or tb > 0:
                        dve.wait_ge(qk_stored[g % 2], tb * 16 * (NQK // 2))
                else:
                    dve.wait_ge(qk_stored[g % 2], tb * 16 * (NQK // 2) + 16 * (g // 2))
                dve.tensor_tensor(qk_out[:, g % 2], acc[:, g % BANKS], rinv_b[:], ALU.mult).then_inc(qk_evacuated, 1)

            dve.wait_ge(gain_loaded, 16)
            split_x(0)
            for i in range(EARLY):
                split_w(i)
            invert(0)
            for g in range(NQK):
                evacuate_qk(0, g)
                for i in range(EARLY + 3 * g, min(EARLY + 3 * g + 3, NPIECE)):
                    split_w(i)
            with dve.Fori(1, NTB) as tb:
                split_x(tb)
                invert(tb)
                for g in range(NQK):
                    evacuate_qk(tb, g)

        @block.tensor
        def _(pe):
            def stats(tb):
                pe.wait_ge(squares_ready, tb + 1)
                if not isinstance(tb, int) or tb > 0:
                    pe.wait_ge(rms_ready, tb)
                for c in range(TB // P):
                    pe.matmul(stat_t[:, c:c + 1], square_sum[:, c * P:(c + 1) * P], ones[:, 0:1], start=True, stop=True)
                pe.matmul(stat_b[:], ones[:], square_sum[:], start=True, stop=True).then_inc(stats_done, 1)

            def group(tb, g):
                evacuated_before(pe, tb, g)
                first = isinstance(tb, int)
                if g < NQK:
                    if first:
                        pe.wait_ge(w_lo_ready, g + 1)
                    for k in range(KD):
                        if g == 0:
                            pe.wait_ge(x_lo_ready, tb * KD + k + 1)
                        cols = slice(g * P, (g + 1) * P)
                        pe.matmul(acc[:, g % BANKS], w_hi[:, k, cols], x_hi[:, k], start=(k == 0), stop=False)
                        pe.matmul(acc[:, g % BANKS], w_hi[:, k, cols], x_lo[:, k], start=False, stop=False)
                        last = pe.matmul(acc[:, g % BANKS], w_lo[:, k, cols], x_hi[:, k], start=False, stop=(k == KD - 1))
                else:
                    e = g - NQK
                    cols = slice(2 * ATT + (e % 2) * ATT, 2 * ATT + (e % 2 + 1) * ATT)
                    if first and e < 2:
                        pe.wait_ge(w_lo_ready, cols.stop // P)
                    rows = slice((e // 2) * P, (e // 2 + 1) * P)
                    for k in range(KD):
                        pe.matmul(acc[:, g % BANKS], x_hi[:, k, rows], w_hi[:, k, cols], start=(k == 0), stop=False)
                        pe.matmul(acc[:, g % BANKS], x_hi[:, k, rows], w_lo[:, k, cols], start=False, stop=False)
                        last = pe.matmul(acc[:, g % BANKS], x_lo[:, k, rows], w_hi[:, k, cols], start=False, stop=(k == KD - 1))
                last.then_inc(group_done, 1)

            pe.wait_ge(consts_ready, 2)
            for g in range(GROUPS):
                if g == 3:
                    stats(0)
                group(0, g)
            with pe.Fori(1, NTB) as tb:
                stats(tb)
                for g in range(GROUPS):
                    group(tb, g)


def phase_attention(nc, lam_in, qk_s, v_s, att_s, total_s):
    NQ = S // P
    QB = TB // P
    NB = NQ // QB
    HALF = S // 2
    SCALE = DH ** -0.5
    CENTER = S - P
    STRIP = CENTER + S
    LAM_INIT = 0.8 - 0.6 * math.exp(0.0)
    STEP0 = int(2.0 ** (-8.0 / H) / SCALE)
    assert STEP0 == 2 and SCALE == 0.125
    with ExitStack() as ctx:
        m = Memory(nc, ctx, "at")
        k_raw = m.sb("k_raw", [P, 2, S])
        k_hi = m.sb("k_hi", [P, 2, S], F32R)
        k_lo = m.sb("k_lo", [P, 2, S], F32R)
        q_raw = m.sb("q_raw", [P, 4, 2, P])
        q_hl = m.sb("q_hl", [P, 2, 2, P], F32R)
        v_main = m.sb("v_main", [P, NQ, P])
        v_last = m.sb("v_last", [P, NQ, P])
        e = m.sb("e", [P, 2, 2, S])
        a_t = m.sb("a_t", [P, 2, NQ, TB])
        bias = m.sb("bias", [P, STRIP], F16)
        ident = m.sb("ident", [P, P])
        ones = m.sb("ones", [P, 1])
        att = m.sb("att", [P, 2, TB])
        att_sq = m.sb("att_sq", [P, TB])
        total = m.sb("total", [P, H * NQ])
        top = m.sb("top", [P, 2, 2, 2])
        neg_top = m.sb("neg_top", [P, 2, 2])
        esum = m.sb("esum", [P, 2, 2])
        coef = m.sb("coef", [P, 2])
        eps_sum = m.sb("eps_sum", [P, NQ])
        lam_v = m.sb("lam_v", [P, 4, DH])
        lam_p = m.sb("lam_p", [P, DH])
        lam_e = m.sb("lam_e", [P, 4])
        neg_lam = m.sb("neg_lam", [P, 1])
        score = m.ps("score", [P, 2, HALF])
        turned = m.ps("turned", [P, 2, TB])
        pv = m.ps("pv", [P, TB])
        stat = m.ps("stat", [P, TB])

        lam_loaded = m.sem("lam_loaded")
        lam_step = m.sem("lam_step")
        lam_exp = m.sem("lam_exp")
        consts_step = m.sem("consts_step")
        distance_ready = m.sem("distance_ready")
        bias_ready = m.sem("bias_ready")
        waited = m.sem("waited")
        k_loaded = m.sem("k_loaded")
        v_main_loaded = m.sem("v_main_loaded")
        v_last_loaded = m.sem("v_last_loaded")
        q_loaded = [m.sem(f"q_loaded{i}") for i in range(4)]
        k_hi_ready = m.sem("k_hi_ready")
        k_lo_ready = m.sem("k_lo_ready")
        q_hi_ready = m.sem("q_hi_ready")
        q_lo_ready = m.sem("q_lo_ready")
        scores_done = m.sem("scores_done")
        biased = m.sem("biased")
        neg_top_ready = m.sem("neg_top_ready")
        exp_done = m.sem("exp_done")
        coef_step = m.sem("coef_step")
        combined = m.sem("combined")
        turned_done = m.sem("turned_done")
        turned_out = m.sem("turned_out")
        pv_done = m.sem("pv_done")
        pv_out = m.sem("pv_out")
        att_sq_ready = m.sem("att_sq_ready")
        stat_done = m.sem("stat_done")
        stat_out = m.sem("stat_out")
        att_stored = [m.sem("att_stored0"), m.sem("att_stored1")]
        total_stored = m.sem("total_stored")
        block = ctx.enter_context(nc.Block())

        def static(x):
            return isinstance(x, int)

        def wait(eng, sem, value):
            if not static(value) or value > 0:
                eng.wait_ge(sem, value)

        def due(h, s, at):
            b = (s - at) // QB
            if (s - at) % QB or (static(h) and h * NB + b < 0):
                return None
            if static(h) and h * NB + b >= H * NB:
                return None
            return b

        @block.sync
        def _(sp):
            sp.dma_start(lam_v[:], lam_in).then_inc(lam_loaded, 16)

            def load_q(h, s):
                n = h * NQ + s
                wait(sp, q_lo_ready, n - 3)
                src = qk_s[bass.ds(h, 1), :, s * P:(s + 1) * P].rearrange("o (c d) t -> (o d) c t", c=2)
                for twin in range(2):
                    sp.dma_start(q_raw[twin * DH:(twin + 1) * DH, s % 4], src).then_inc(q_loaded[s % 4], 16)

            def load_k(h):
                wait(sp, k_lo_ready, 8 * h)
                src = qk_s[bass.ds(h + H, 1)].rearrange("o (c d) t -> (o d) c t", c=2)
                for twin in range(2):
                    sp.dma_start(k_raw[twin * DH:(twin + 1) * DH], src).then_inc(k_loaded, 16)

            def load_v(h, dst, sem):
                src = v_s[:, bass.ds(h * P, P)].rearrange("(k p) c -> p k c", p=P)
                sp.dma_start(dst[:], src).then_inc(sem, 16)

            def store(h, s):
                b = due(h, s, 10 + 4)
                if b is not None:
                    g = h * NB + b
                    sp.wait_ge(pv_out, g + 1)
                    hb = h if b >= 0 else h - 1
                    sp.dma_start(att_s[bass.ds(hb, 1), :, (b % NB) * TB:(b % NB + 1) * TB].rearrange("o p t -> (o p) t"),
                                 att[:, b % 2]).then_inc(att_stored[b % 2], 16)

            def head(h):
                load_k(h)
                for s in range(NQ):
                    load_q(h, s)
                    if s == 2:
                        wait(sp, pv_done, h * NB - 1)
                        load_v(h, v_main, v_main_loaded)
                    if s == 9:
                        wait(sp, pv_done, h * NB)
                        load_v(h, v_last, v_last_loaded)
                    store(h, s)

            head(0)
            with sp.Fori(1, H) as h:
                head(h)
            for s in range(QB * 4 + 1):
                store(H, s)
            for i in range(2):
                sp.wait_ge(att_stored[i], 16 * H * NB // 2)
            sp.wait_ge(stat_out, H * NB)
            sp.dma_start(total_s.rearrange("p h t -> p (h t)"), total[:]).then_inc(total_stored, 16)
            sp.wait_ge(total_stored, 16)

        @block.gpsimd
        def _(pool):
            pool.memset(ident[:], 0.0).then_inc(consts_step, 1)
            pool.memset(ones[:], 1.0).then_inc(consts_step, 1)
            distance = e[:].rearrange("p a c t -> p (a c t)")[:, 0:STRIP].bitcast(I32)
            pool.iota(distance, pattern=[[-STEP0, STRIP]], base=STEP0 * CENTER, channel_multiplier=STEP0).then_inc(distance_ready, 1)
            pool.wait_ge(consts_step, 2)
            pool.affine_select(out=ident[:], in_=ident[:], compare_op=ALU.not_equal, fill=1.0, base=0,
                               pattern=[[-1, P]], channel_multiplier=1).then_inc(consts_step, 1)
            with pool.Fori(0, H * NB // 2) as pair:
                for slot in range(2):
                    g = pair * 2 + slot
                    pool.wait_ge(pv_out, g + 1)
                    pool.tensor_tensor(att_sq[:], att[:, slot], att[:, slot], ALU.mult).then_inc(att_sq_ready, 1)
                    pool.wait_ge(stat_done, g + 1)

        @block.scalar
        def _(act):
            def q_high(h, s):
                n = h * NQ + s
                act.wait_ge(q_loaded[s % 4], 32 * (h * (NQ // 4) + s // 4 + 1))
                wait(act, scores_done, 4 * (n - 1))
                act.activation(q_hl[:, s % 2], q_raw[:, s % 4], ACT.Copy).then_inc(q_hi_ready, 1)

            def k_high(h):
                act.wait_ge(k_loaded, 32 * (h + 1))
                wait(act, scores_done, 4 * NQ * h)
                for c in range(2):
                    for quarter in range(4):
                        cols = bass.ts(quarter, TB)
                        act.activation(k_hi[:, c, cols], k_raw[:, c, cols], ACT.Copy).then_inc(k_hi_ready, 1)

            def exponential(h, s, c):
                n = h * NQ + s
                act.wait_ge(neg_top_ready, 2 * n + c + 1)
                act.activation(e[:, s % 2, c], e[:, s % 2, c], ACT.Exp, bias=neg_top[:, s % 2, c:c + 1], scale=SCALE,
                               accum_out=esum[:, s % 2, c:c + 1]).then_inc(exp_done, 1)

            def copy_turned(h, s, js):
                n = h * NQ + s
                if static(n) and n <= 0:
                    return
                b, col = (s - 1) // QB, (s - 1) % QB
                if col == 0 and js[0] == 0:
                    wait(act, pv_done, h * NB + b - 1)
                for j in js:
                    act.wait_ge(turned_done, 4 * (n - 1) + j + 1)
                    act.activation(a_t[:, b % 2, 4 * j:4 * j + 4, col * P:(col + 1) * P],
                                   turned[:, j % 2].rearrange("p (k q) -> p k q", q=P), ACT.Copy).then_inc(turned_out, 1)

            def copy_results(h, s):
                b = due(h, s, 9)
                if b is not None:
                    g = h * NB + b
                    act.wait_ge(pv_done, g + 1)
                    wait(act, att_stored[b % 2], 16 * (h * (NB // 2) + b // 2))
                    wait(act, att_sq_ready, g - 1)
                    act.activation(att[:, b % 2], pv[:], ACT.Copy).then_inc(pv_out, 1)
                b = due(h, s, 11)
                if b is not None:
                    g = h * NB + b
                    act.wait_ge(stat_done, g + 1)
                    act.activation(total[:, bass.ds(g * QB, QB)], stat[:, 0:QB], ACT.Copy).then_inc(stat_out, 1)

            def head(h):
                q_high(h, 0)
                k_high(h)
                for s in range(NQ):
                    if s + 1 < NQ:
                        q_high(h, s + 1)
                    copy_turned(h, s - 1, (2, 3))
                    exponential(h, s, 0)
                    copy_results(h, s)
                    copy_turned(h, s, (0, 1))
                    exponential(h, s, 1)

            act.wait_ge(lam_step, 2)
            act.activation(lam_e[:, 2:4], lam_e[:, 0:2], ACT.Exp).then_inc(lam_exp, 1)
            head(0)
            with act.Fori(1, H) as h:
                head(h)
            copy_turned(H, -1, (2, 3))
            copy_turned(H, 0, (0, 1))
            copy_turned(H, 0, (2, 3))
            for s in range(3 * QB):
                copy_results(H, s)

        @block.vector
        def _(dve):
            def q_low(h, s):
                n = h * NQ + s
                dve.wait_ge(q_hi_ready, n + 1)
                low = q_hl[DH:P, s % 2]
                dve.tensor_tensor(low, q_raw[DH:P, s % 4], low.bitcast(F32), ALU.subtract).then_inc(q_lo_ready, 1)

            def k_low(h):
                for c in range(2):
                    for quarter in range(4):
                        dve.wait_ge(k_hi_ready, 8 * h + 4 * c + quarter + 1)
                        cols = bass.ts(quarter, TB)
                        dve.tensor_tensor(k_lo[:, c, cols], k_raw[:, c, cols], k_hi[:, c, cols].bitcast(F32),
                                          ALU.subtract).then_inc(k_lo_ready, 1)

            def add_bias(h, s, c, half):
                n = h * NQ + s
                hf = 2 * c + half
                if c == 0:
                    wait(dve, turned_done, 4 * (n - 2) + 2 * half + 2)
                dve.wait_ge(scores_done, 4 * n + hf + 1)
                if half:
                    dve.wait_ge(biased, 4 * n + hf)
                dve.sem_inc(waited, 1)
                at = CENTER - s * P + half * HALF
                dve.tensor_tensor_reduce(
                    out=e[:, s % 2, c, half * HALF:(half + 1) * HALF], in0=score[:, half], in1=bias[:, at:at + HALF],
                    scale=1.0, scalar=top[:, s % 2, c, 0:1] if half else -3.0e38, op0=ALU.add, op1=ALU.max,
                    accum_out=top[:, s % 2, c, half:half + 1]).then_inc(biased, 1)

            def negate_top(h, s, c):
                n = h * NQ + s
                dve.wait_ge(biased, 4 * n + 2 * c + 2)
                dve.tensor_scalar(neg_top[:, s % 2, c:c + 1], top[:, s % 2, c, 1:2], -SCALE, None, ALU.mult)\
                    .then_inc(neg_top_ready, 1)

            def combine(h, s, part):
                n = h * NQ + s
                if static(n) and n == 0:
                    return
                slot = (s - 1) % 2
                if part == 0:
                    dve.wait_ge(exp_done, 2 * n)
                    if (s - 1) % QB == 0:
                        wait(dve, stat_done, h * NB + (s - 1) // QB - NB + 1)
                    at = (s - 1) % NQ
                    dve.reciprocal(coef[:, 0:1], esum[:, slot, 1:2]).then_inc(coef_step, 1)
                    dve.scalar_tensor_tensor(eps_sum[:, at:at + 1], esum[:, slot, 0:1], P * EPS, esum[:, slot, 0:1],
                                             ALU.mult, ALU.mult)
                elif part == 1:
                    dve.wait_ge(coef_step, 2 * n - 1)
                    dve.scalar_tensor_tensor(coef[:, 1:2], esum[:, slot, 0:1], neg_lam[:, 0:1], coef[:, 0:1],
                                             ALU.mult, ALU.mult).then_inc(coef_step, 1)
                else:
                    dve.wait_ge(coef_step, 2 * n)
                    dve.scalar_tensor_tensor(e[:, slot, 0], e[:, slot, 1], coef[:, 1:2], e[:, slot, 0],
                                             ALU.mult, ALU.add).then_inc(combined, 1)

            def head(h):
                if not static(h):
                    dve.tensor_scalar(bias[:], bias[:], 0.25, None, ALU.mult).then_inc(bias_ready, 1)
                q_low(h, 0)
                k_low(h)
                dve.wait_ge(bias_ready, h + 1)
                for s in range(NQ):
                    add_bias(h, s, 0, 0)
                    add_bias(h, s, 0, 1)
                    combine(h, s, 0)
                    negate_top(h, s, 0)
                    combine(h, s, 1)
                    if s + 1 < NQ:
                        q_low(h, s + 1)
                    combine(h, s, 2)
                    add_bias(h, s, 1, 0)
                    add_bias(h, s, 1, 1)
                    negate_top(h, s, 1)

            dve.wait_ge(lam_loaded, 16)
            for i in range(2):
                if i:
                    dve.wait_ge(lam_step, 1)
                dve.tensor_tensor_reduce(out=lam_p[:], in0=lam_v[:, 2 * i], in1=lam_v[:, 2 * i + 1], scale=1.0, scalar=0.0,
                                         op0=ALU.mult, op1=ALU.add, accum_out=lam_e[:, i:i + 1]).then_inc(lam_step, 1)
            dve.wait_ge(distance_ready, 1)
            distance = e[:].rearrange("p a c t -> p (a c t)")[:, 0:STRIP].bitcast(I32)
            dve.scalar_tensor_tensor(bias[:], distance, -1.0, distance, ALU.mult, ALU.min).then_inc(bias_ready, 1)
            dve.wait_ge(lam_exp, 1)
            dve.tensor_tensor(neg_lam[:], lam_e[:, 3:4], lam_e[:, 2:3], ALU.subtract).then_inc(lam_step, 1)
            dve.wait_ge(lam_step, 3)
            dve.tensor_scalar(neg_lam[:], neg_lam[:], LAM_INIT, None, ALU.subtract).then_inc(lam_step, 1)
            dve.wait_ge(lam_step, 4)
            head(0)
            with dve.Fori(1, H) as h:
                head(h)
            for part in range(3):
                combine(H, 0, part)

        @block.tensor
        def _(pe):
            def scores(h, s, hf):
                n = h * NQ + s
                c, half = hf // 2, hf % 2
                if hf == 0:
                    pe.wait_ge(q_lo_ready, n + 1)
                if s == 0:
                    pe.wait_ge(k_lo_ready, 8 * h + 2 * (hf + 1))
                wait(pe, biased, 4 * n + hf - 1)
                for bank in range(HALF // TB):
                    cols = slice(half * HALF + bank * TB, half * HALF + (bank + 1) * TB)
                    out = score[:, half, bank * TB:(bank + 1) * TB]
                    pe.matmul(out, q_hl[:, s % 2, c], k_hi[:, c, cols], start=True, stop=False)
                    last = pe.matmul(out, q_hl[:, s % 2, c], k_lo[:, c, cols], start=False, stop=True)
                last.then_inc(scores_done, 1)

            def values(h, s, part):
                b, j = (s - 6) // QB, (s - 6) % QB
                if static(h) and not 0 <= h * NB + b < H * NB:
                    return
                g = h * NB + b
                if j == 0 and part == 0:
                    pe.wait_ge(turned_out, 16 * (g + 1))
                    wait(pe, pv_out, g)
                    if b == -1:
                        pe.wait_ge(v_last_loaded, 16 * h)
                    if b == 0:
                        pe.wait_ge(v_main_loaded, 16 * (h + 1))
                v = v_last if b == -1 else v_main
                kt = 4 * j + part
                last = pe.matmul(pv[:], v[:, kt], a_t[:, b % 2, kt], start=(kt == 0), stop=(kt == NQ - 1))
                if kt == NQ - 1:
                    last.then_inc(pv_done, 1)

            def turn(h, s, j):
                n = h * NQ + s
                if static(n) and n <= 0:
                    return
                if j == 0:
                    pe.wait_ge(combined, n)
                wait(pe, turned_out, 4 * (n - 1) + j - 1)
                for i in range(4):
                    kt = 4 * j + i
                    last = pe.transpose(turned[:, j % 2, i * P:(i + 1) * P], e[:, (s - 1) % 2, 0, kt * P:(kt + 1) * P],
                                        ident[:])
                last.then_inc(turned_done, 1)

            def statistics(h, s):
                b = due(h, s, 10)
                if b is None:
                    return
                g = h * NB + b
                pe.wait_ge(att_sq_ready, g + 1)
                wait(pe, stat_out, g)
                for c in range(QB):
                    pe.matmul(stat[:, c:c + 1], att_sq[:, c * P:(c + 1) * P], ones[:],
                              start=(c == 0), stop=False, skip_group_check=True)
                at = (b % NB) * QB
                last = pe.matmul(stat[:, 0:QB], ident[:], eps_sum[:, at:at + QB], start=False, stop=True,
                                 skip_group_check=True)
                last.then_inc(stat_done, 1)

            def step(h, s):
                scores(h, s, 0)
                turn(h, s - 1, 2)
                turn(h, s - 1, 3)
                scores(h, s, 1)
                values(h, s, 0)
                values(h, s, 1)
                scores(h, s, 2)
                values(h, s, 2)
                scores(h, s, 3)
                values(h, s, 3)
                turn(h, s, 0)
                turn(h, s, 1)
                statistics(h, s)

            pe.wait_ge(consts_step, 3)
            for s in range(NQ):
                step(0, s)
            with pe.Fori(1, H) as h:
                for s in range(NQ):
                    step(h, s)
            turn(H, -1, 2)
            turn(H, -1, 3)
            for j in range(4):
                turn(H, 0, j)
            for s in range(3 * QB):
                for part in range(4):
                    values(H, s, part)
                statistics(H, s)


def phase_ssm(nc, s_par, s_d, s_bc, w_glu, b_glu, u_s, ssm_s):
    T = 8
    NJ = S // T
    G = 8
    GH = 16
    PAIRS = 2 * G
    NQU = 4
    N = 64
    NDG = NQU * PAIRS
    JB = NJ // P
    BATCH = 2
    XR = 6
    MAG, THETA, A_RE, A_IM, E_RE, E_IM, NPAR = 0, 1, 2, 2 + T + 1, 4 + 2 * T, 4 + 3 * T, 4 + 4 * T
    MAGIC = 1.5 * 2.0 ** 23
    TURN = 2.0 * math.pi
    C1 = 6.28125
    C2 = float(np.float32(math.floor((TURN - C1) * 2.0 ** 22) / 2.0 ** 22))
    C3 = float(np.float32(TURN - C1 - C2))
    PI_BELOW = 3.1415925
    with ExitStack() as ctx:
        m = Memory(nc, ctx, "sm")
        par = m.sb("par", [P, NPAR, NDG])
        par_q = m.sb("par_q", [P, E_RE, PAIRS])
        input_q = m.sb("input_q", [P, 2 * T, PAIRS])
        theta_q = m.sb("theta_q", [P, 1, PAIRS])
        bc = m.sb("bc", [P, 4, PAIRS, GH])
        bp = m.sb("bp", [P, PAIRS, T, GH])
        cp = m.sb("cp", [P, PAIRS, T + 1, GH])
        cp_swap = m.sb("cp_swap", [P, PAIRS, T + 1, GH])
        part = m.sb("part", [P, PAIRS, T, GH])
        strip = m.sb("strip", [GH, G, 2 * T - 1, GH])
        toeplitz = m.sb("toeplitz", [P, G, P])
        p_t = m.sb("p_t", [P, PAIRS, 3 * N])
        u_raw = m.sb("u_raw", [P, JB, T, P])
        uz = m.sb("uz", [P, JB, T * P])
        u_t = m.sb("u_t", [P, G, NJ])
        tab = m.sb("tab", [P, PAIRS, 2, NJ])
        cycles = m.sb("cycles", [P, PAIRS, NJ])
        whole = m.sb("whole", [P, BATCH, NJ])
        half_sine = m.sb("half_sine", [P, 2, BATCH, NJ])
        turned_w = m.sb("turned_w", [P, 2, 2, NJ])
        scan_in = m.sb("scan_in", [P, 2, NJ])
        scan_out = m.sb("scan_out", [P, 2, NJ])
        x_st = m.sb("x_st", [P, XR, 2, NJ + 1])
        z_t = m.sb("z_t", [P, NQU, S])
        wg = u_raw[:].rearrange("p b s c -> p (b s c)").rearrange("p (k n) -> p k n", k=4)
        bg = m.sb("bg", [P, 4])
        chunk = m.sb("chunk", [P, NJ])
        sign = m.sb("sign", [P, 3])
        ident = m.sb("ident", [P, P])
        d_in = m.sb("d_in", [GH, NDG // 2])
        d_diag = m.sb("d_diag", [GH, NDG // 2, GH])
        d_q = m.sb("d_q", [GH, G, GH])
        gate = tab[:].rearrange("p a c t -> p (a c t)")[:, 0:2 * TB].rearrange("p (r t) -> p r t", r=2)
        out = tab[:].rearrange("p a c t -> p (a c t)")[:, 2 * TB:4 * TB].rearrange("p (r t) -> p r t", r=2)
        w_ps = m.ps("w_ps", [P, 2, 2, NJ])
        y_ps = m.ps("y_ps", [P, 2, TB])
        turn_ps = m.ps("turn_ps", [P, 2, TB])
        lag_ps = m.ps("lag_ps", [P, 2, TB])

        const_loaded = m.sem("const_loaded")
        const_step = m.sem("const_step")
        prep = m.sem("prep")
        wg_loaded = m.sem("wg_loaded")
        prep_act = m.sem("prep_act")
        waited = m.sem("waited")
        bc_loaded = m.sem("bc_loaded")
        u_loaded = m.sem("u_loaded")
        ug_ready = m.sem("ug_ready")
        par_q_ready = m.sem("par_q_ready")
        input_q_ready = m.sem("input_q_ready")
        b_signed = m.sem("b_signed")
        b_product = m.sem("b_product")
        square_ready = m.sem("square_ready")
        theta_q_ready = m.sem("theta_q_ready")
        angle_ready = m.sem("angle_ready")
        whole_ready = m.sem("whole_ready")
        product_step = m.sem("product_step")
        bp_ready = m.sem("bp_ready")
        cp_ready = m.sem("cp_ready")
        swap_loaded = m.sem("swap_loaded")
        lag_done = m.sem("lag_done")
        strip_step = m.sem("strip_step")
        strip_side = m.sem("strip_side")
        toeplitz_loaded = [m.sem("toeplitz_loaded0"), m.sem("toeplitz_loaded1")]
        turn_done = m.sem("turn_done")
        turn_out = m.sem("turn_out")
        cycles_ready = m.sem("cycles_ready")
        sines_ready = m.sem("sines_ready")
        tab_ready = m.sem("tab_ready")
        w_done = m.sem("w_done")
        turned_ready = m.sem("turned_ready")
        scan_in_ready = m.sem("scan_in_ready")
        scanned = m.sem("scanned")
        x_ready = m.sem("x_ready")
        ug_half = m.sem("ug_half")
        p_half = m.sem("p_half")
        bc_signed = m.sem("bc_signed")
        phase_act = m.sem("phase_act")
        edges_ready = m.sem("edges_ready")
        y_done = m.sem("y_done")
        z_ready = m.sem("z_ready")
        glu_done = m.sem("glu_done")
        gate_ready = m.sem("gate_ready")
        out_ready = m.sem("out_ready")
        out_stored = [m.sem("out_stored0"), m.sem("out_stored1")]
        block = ctx.enter_context(nc.Block())

        DT, LR, ANG, MG, MG8, KK, RR, SN, SH, TH, NR, DEN, CR, CI, NCOL = range(15)
        PREP_LR, PREP_R, PREP_END = 2, 8, 68

        def scr(t, i, n=1):
            flat = t[:].rearrange("p a c t -> p (a c t)")[:, i * NDG:(i + n) * NDG]
            return flat if n == 1 else flat.rearrange("p (n d) -> p n d", n=n)

        def scr_block(t, i, a, n):
            return scr(t, i, a * n).rearrange("p (a n) d -> p a n d", a=a)

        def pair(i):
            return (i % 2) * G + i // 2

        def x_slot(i):
            return i % XR

        U_TURNS, B_TURNS, Z_TURNS = 4, 4, 4
        QT = U_TURNS + B_TURNS + Z_TURNS

        def tail(q):
            return U_TURNS + B_TURNS + q * QT

        def u_turn(q):
            return 0 if static(q) and q == 0 else tail(q - 1) + B_TURNS + Z_TURNS

        def b_turn(q):
            return U_TURNS if static(q) and q == 0 else tail(q - 1)

        def z_turn(q, last):
            return tail(q) + (0 if last else B_TURNS)

        BATCHES = PAIRS // BATCH
        ORDER = [b for g in range(BATCHES // 2) for b in (g, g + BATCHES // 2)]

        def batch_pairs(i):
            return slice(ORDER[i] * BATCH, (ORDER[i] + 1) * BATCH)

        def tab_used(i):
            b = ORDER[i]
            return 2 * (BATCH * (b % (BATCHES // 2)) + BATCH - 1) + b // (BATCHES // 2) + 1

        def batch_of(i):
            return (i // (2 * BATCH)) * 2 + i % 2
        u_chunks = u_s.rearrange("(b j s) c -> j b s c", b=JB, s=T)
        first_chunk = uz[:].rearrange("p b (s c) -> p b s c", s=T)

        def static(x):
            return isinstance(x, int)

        def wait(eng, sem, value):
            if not static(value) or value > 0:
                eng.wait_ge(sem, value)

        def quarters(eng, body):
            body(0, False)
            with eng.Fori(1, NQU - 1) as q:
                body(q, False)
            body(NQU - 1, True)

        def outer(eng, dst, tmp, coefs, re, im, n, src, step, done):
            shape = [P, PAIRS, n, GH]

            def coef(i):
                return coefs[:, i:i + n].rearrange("p n d -> p d n").unsqueeze(3).to_broadcast(shape)

            eng.tensor_tensor(dst, coef(re), bc[:, src].unsqueeze(2).to_broadcast(shape), ALU.mult).then_inc(step, 1)
            eng.tensor_tensor(tmp, coef(im), bc[:, src + 1].unsqueeze(2).to_broadcast(shape), ALU.mult).then_inc(step, 1)
            eng.wait_ge(step, done + 2)
            return eng.tensor_tensor(dst, dst, tmp, ALU.subtract)

        def make_b(eng, q):
            wait(eng, bp_ready, q)
            eng.tensor_copy(input_q[:], par[:, E_RE:NPAR, bass.ds(q * PAIRS, PAIRS)]).then_inc(input_q_ready, 1)
            eng.wait_ge(input_q_ready, q + 1)
            eng.wait_ge(bc_loaded, 16 * q + 16)
            eng.sem_inc(waited, 1)
            eng.tensor_scalar(bc[:, 1], bc[:, 1], sign[:, 0:1], None, ALU.mult).then_inc(b_signed, 1)
            eng.wait_ge(b_signed, q + 1)
            outer(eng, bp[:], part[:], input_q, 0, T, T, 0, b_product, 2 * q).then_inc(bp_ready, 1)

        @block.sync
        def _(sp):
            sp.dma_start(par[:, 0:3], s_par).then_inc(const_loaded, 16)
            sp.dma_start(d_in[:], s_d).then_inc(const_loaded, 16)
            sp.dma_start(bg[:], b_glu).then_inc(const_loaded, 16)

            def body(q, last):
                wait(sp, bp_ready, q)
                wait(sp, cp_ready, q)
                sp.dma_start(bc[:], s_bc[bass.ds(q, 1)].rearrange("o p a b c -> (o p) a b c")).then_inc(bc_loaded, 16)
                wait(sp, ug_ready, q)
                for b in range(JB):
                    sp.dma_start(u_raw[:, b], u_chunks[:, b, :, bass.ds(q * P, P)]).then_inc(u_loaded, 16)
                wait(sp, y_done, q * G)
                sp.sem_inc(waited, 1)
                sp.wait_ge(cp_ready, q + 1)
                for h in range(2):
                    sp.dma_start(cp_swap[(1 - h) * N:(2 - h) * N], cp[h * N:(h + 1) * N]).then_inc(swap_loaded, 16)
                for half in range(2):
                    sp.wait_ge(strip_step, 6 * q + 3 * half + 3)
                    gs = slice(half * 4, half * 4 + 4)
                    for s in range(T):
                        sp.dma_start(toeplitz[s * GH:(s + 1) * GH, gs].rearrange("p g (s h) -> p g s h", s=T),
                                     strip[:, gs, T - 1 - s:2 * T - 1 - s]).then_inc(toeplitz_loaded[half], 16)

            quarters(sp, body)
            sp.wait_ge(ug_ready, NQU)
            sp.dma_start(wg, w_glu).then_inc(wg_loaded, 16)
            for n in range(4 * NTB):
                tb, c = n // 4, n % 4
                sp.wait_ge(out_ready, n + 1)
                sp.dma_start(ssm_s[c, :, tb * TB:(tb + 1) * TB], out[:, n % 2]).then_inc(out_stored[n % 2], 16)
            for i in range(2):
                sp.wait_ge(out_stored[i], 16 * 2 * NTB)

        @block.gpsimd
        def _(pool):
            pool.memset(ident[:], 0.0).then_inc(const_step, 1)
            chunk_i = whole[:, 0].bitcast(I32)
            pool.iota(chunk_i, pattern=[[1, NJ]], base=0, channel_multiplier=0).then_inc(const_step, 1)
            for h, s in ((0, 1.0), (1, -1.0)):
                rows = slice(h * N, (h + 1) * N)
                pool.wait_ge(const_step, 2 + 2 * h)
                pool.memset(sign[rows, 0:1], s).then_inc(const_step, 1)
                pool.memset(sign[rows, 1:2], s * 2 * PI_BELOW).then_inc(const_step, 1)
            pool.wait_ge(const_step, 6)
            pool.affine_select(out=ident[:], in_=ident[:], compare_op=ALU.not_equal, fill=1.0, base=0,
                               pattern=[[-1, P]], channel_multiplier=1).then_inc(const_step, 1)
            pool.tensor_copy(chunk[:], chunk_i).then_inc(const_step, 1)

            def make_cycles(q):
                n = q * BATCHES
                wait(pool, cycles_ready, n)
                pool.tensor_copy(theta_q[:], par[:, THETA:THETA + 1, bass.ds(q * PAIRS, PAIRS)]).then_inc(theta_q_ready, 1)
                pool.wait_ge(theta_q_ready, q + 1)

                def angles(i):
                    wait(pool, sines_ready, n - BATCHES + i + 1)
                    shape = [P, BATCH, NJ]
                    pairs = batch_pairs(i)
                    pool.tensor_tensor(cycles[:, pairs], chunk[:].unsqueeze(1).to_broadcast(shape),
                                       theta_q[:, 0, pairs].unsqueeze(2).to_broadcast(shape), ALU.mult).then_inc(angle_ready, 1)

                def take_off(i):
                    pool.wait_ge(whole_ready, n + i + 1)
                    mine = cycles[:, batch_pairs(i)]
                    pool.tensor_tensor(mine, mine, whole[:], ALU.subtract).then_inc(cycles_ready, 1)

                if static(q) and q == 0:
                    angles(0)
                    for i in range(BATCHES):
                        if i + 1 < BATCHES:
                            angles(i + 1)
                        take_off(i)
                    return
                for i in range(BATCHES // 2):
                    angles(i)
                pool.wait_ge(lag_done, 2 * q)
                make_b(pool, q)
                for i in range(BATCHES // 2, BATCHES):
                    angles(i)
                for i in range(BATCHES):
                    take_off(i)

            pool.wait_ge(const_step, 8)
            pool.wait_ge(prep, PREP_END)
            make_cycles(0)
            with pool.Fori(1, NQU) as q:
                make_cycles(q)

        @block.scalar
        def _(act):
            def turn_end(turn):
                act.wait_ge(turn_done, turn + 1)
                act.sem_inc(waited, 1)

            act.wait_ge(const_loaded, 48)
            act.activation(scr(tab, DT), par[:, 2], ACT.Exp).then_inc(prep_act, 1)
            act.wait_ge(prep, PREP_LR)
            act.activation(scr(tab, MG), scr(tab, LR), ACT.Exp)
            act.activation(scr(tab, MG8), scr(tab, LR), ACT.Exp, scale=float(T)).then_inc(prep_act, 1)
            act.wait_ge(prep, PREP_R)
            act.activation(scr(tab, SN), scr(tab, RR), ACT.Sin)
            act.activation(scr(tab, SH), scr(tab, RR), ACT.Sin, scale=0.5).then_inc(prep_act, 1)

            def turned_b(q):
                wait(act, w_done, q * PAIRS)
                for t in range(B_TURNS):
                    turn_end(b_turn(q) + t)
                    src = turn_ps[:, t % 2].rearrange("p (g n) -> p g n", g=4)
                    act.activation(p_t[:, 4 * t:4 * t + 4, 0:P], src, ACT.Copy).then_inc(p_half, 1)
                    act.activation(p_t[:, 4 * t:4 * t + 4, P:3 * N], src[:, :, 0:N], ACT.Copy).then_inc(p_half, 1)
                    act.wait_ge(p_half, q * 2 * B_TURNS + 2 * t + 2)
                    act.sem_inc(turn_out, 1)

            def sines(q, i):
                n = q * BATCHES + i
                b = ORDER[i]
                act.wait_ge(cycles_ready, n + 1)
                wait(act, x_ready, (q - 1) * PAIRS + tab_used(i) if not static(q) or q else 0)
                pairs = slice(b * BATCH, (b + 1) * BATCH)
                hs = half_sine[:, i % 2]
                wait(act, tab_ready, n - 1)
                act.activation(hs, cycles[:, pairs], ACT.Sin, scale=PI_BELOW).then_inc(phase_act, 1)
                act.activation(tab[:, pairs, 1], cycles[:, pairs], ACT.Sin, scale=sign[:, 1:2]).then_inc(sines_ready, 1)
                act.wait_ge(phase_act, n + 1)
                act.activation(hs, hs, ACT.Square, scale=math.sqrt(2.0)).then_inc(square_ready, 1)
                act.wait_ge(square_ready, n + 1)
                act.activation(tab[:, pairs, 0], hs, ACT.Copy, scale=-1.0, bias=1.0).then_inc(tab_ready, 1)

            def regroup_u(q):
                act.wait_ge(u_loaded, 16 * JB * (q + 1))
                wait(act, turn_done, u_turn(q))
                for b in range(JB):
                    act.activation(uz[:, b].rearrange("p (g s h) -> p s g h", g=G, s=T),
                                   u_raw[:, b].rearrange("p s (g h) -> p s g h", g=G), ACT.Copy).then_inc(ug_half, 1)
                act.wait_ge(ug_half, JB * (q + 1))
                act.sem_inc(ug_ready, 1)

            def turned_u(q):
                wait(act, y_done, q * G)
                for t in range(U_TURNS):
                    turn_end(u_turn(q) + t)
                    act.activation(u_t[:, 2 * t:2 * t + 2], turn_ps[:, t % 2].rearrange("p (g j) -> p g j", g=2),
                                   ACT.Copy).then_inc(turn_out, 1)

            def body(q, last):
                for i in range(2, BATCHES):
                    sines(q, i)
                for g in range(G):
                    act.wait_ge(y_done, q * G + g + 1)
                    act.activation(first_chunk[:, :, :, g * GH:(g + 1) * GH],
                                   y_ps[:, g % 2, 0:JB * P].rearrange("p (b s h) -> p b s h", b=JB, s=T),
                                   ACT.Gelu).then_inc(z_ready, 1)
                    if g == G // 2 and not last:
                        for i in range(2):
                            sines(q + 1, i)
                    if g == G - 3 and not last:
                        turned_b(q + 1)
                for t in range(Z_TURNS):
                    if t == 2 and not last:
                        regroup_u(q + 1)
                    turn_end(z_turn(q, last) + t)
                    b, s4 = t // 2, t % 2
                    dst = z_t[:, bass.ds(q, 1)].rearrange("p o (b j s) -> p (o b) s j", b=JB, s=T)
                    act.activation(dst[:, b, 4 * s4:4 * s4 + 4], turn_ps[:, t % 2].rearrange("p (s j) -> p s j", s=4),
                                   ACT.Copy).then_inc(turn_out, 1)
                if not last:
                    turned_u(q + 1)

            regroup_u(0)
            turned_u(0)
            act.wait_ge(prep, PREP_END)
            sines(0, 0)
            sines(0, 1)
            turned_b(0)
            quarters(act, body)
            for n in range(4 * NTB):
                act.wait_ge(glu_done, n + 1)
                wait(act, out_ready, n - 1)
                act.activation(gate[:, n % 2], y_ps[:, n % 2], ACT.Sigmoid, bias=bg[:, n % 4:n % 4 + 1])\
                    .then_inc(gate_ready, 1)

        @block.vector
        def _(dve):
            steps = [0]

            def then(instruction):
                instruction.then_inc(prep, 1)
                steps[0] += 1
                dve.wait_ge(prep, steps[0])

            def col(i):
                return scr(tab, i)

            def tt(o, a, b, op):
                then(dve.tensor_tensor(o, a, b, op))

            def reduce(r, x, k, inv_period, c1, c2, c3):
                then(dve.tensor_scalar(k, x, inv_period, MAGIC, ALU.mult, ALU.add))
                then(dve.tensor_scalar(k, k, MAGIC, None, ALU.subtract))
                then(dve.scalar_tensor_tensor(r, k, -c1, x, ALU.mult, ALU.add))
                then(dve.scalar_tensor_tensor(r, k, -c2, r, ALU.mult, ALU.add))
                then(dve.scalar_tensor_tensor(r, k, -c3, r, ALU.mult, ALU.add))

            def complex_mult(o_re, o_im, a_re, a_im, b_re, b_im, tmp):
                tt(tmp, a_im, b_im, ALU.mult)
                tt(o_re, a_re, b_re, ALU.mult)
                tt(o_re, o_re, tmp, ALU.subtract)
                tt(tmp, a_im, b_re, ALU.mult)
                tt(o_im, a_re, b_im, ALU.mult)
                tt(o_im, o_im, tmp, ALU.add)

            def parameters():
                re, im = par[:, 0], par[:, 1]
                dve.wait_ge(const_loaded, 48)
                dve.wait_ge(prep_act, 1)
                tt(col(LR), re, col(DT), ALU.mult)
                tt(col(ANG), im, col(DT), ALU.mult)
                assert steps[0] == PREP_LR
                reduce(col(RR), col(ANG), col(KK), 1.0 / TURN, C1, C2, C3)
                then(dve.tensor_scalar(col(RR), col(RR), PI_BELOW, -PI_BELOW, ALU.min, ALU.max))
                assert steps[0] == PREP_R
                reduce(col(TH), col(RR), col(KK), T / TURN, C1 / T, C2 / T, C3 / T)
                then(dve.tensor_scalar(col(TH), col(TH), T / TURN, None, ALU.mult))
                dve.wait_ge(prep_act, 3)
                powers, inputs = scr_block(tab, NCOL, 2, T + 1), scr_block(tab, NCOL + 2 * T + 2, 2, T)
                tmp = scr_block(tab, NCOL + 4 * T + 2, 1, T)[:, 0]
                then(dve.scalar_tensor_tensor(col(KK), col(SH), -2.0, col(SH), ALU.mult, ALU.mult))
                then(dve.tensor_scalar(col(KK), col(KK), 1.0, None, ALU.add))
                tt(powers[:, 0, 1], col(KK), col(MG), ALU.mult)
                tt(powers[:, 1, 1], col(SN), col(MG), ALU.mult)
                then(dve.memset(powers[:, 0, 0], 1.0))
                then(dve.memset(powers[:, 1, 0], 0.0))
                for have in (1, 2, 4):
                    a, b = powers[:, :, have], powers[:, :, 1:have + 1]
                    o = powers[:, :, have + 1:2 * have + 1]
                    by = [a[:, i].unsqueeze(1).to_broadcast([P, have, NDG]) for i in range(2)]
                    complex_mult(o[:, 0], o[:, 1], by[0], by[1], b[:, 0], b[:, 1], tmp[:, 0:have])
                ar, ai = powers[:, 0, 1], powers[:, 1, 1]
                then(dve.tensor_scalar(col(NR), ar, 1.0, None, ALU.subtract))
                tt(col(KK), re, re, ALU.mult)
                tt(col(DEN), im, im, ALU.mult)
                tt(col(DEN), col(DEN), col(KK), ALU.add)
                then(dve.reciprocal(col(DEN), col(DEN)))
                tt(col(CR), col(NR), re, ALU.mult)
                tt(col(KK), ai, im, ALU.mult)
                tt(col(CR), col(CR), col(KK), ALU.add)
                tt(col(CR), col(CR), col(DEN), ALU.mult)
                tt(col(CI), ai, re, ALU.mult)
                tt(col(KK), col(NR), im, ALU.mult)
                tt(col(CI), col(CI), col(KK), ALU.subtract)
                tt(col(CI), col(CI), col(DEN), ALU.mult)
                cr, ci = (col(i).unsqueeze(1).to_broadcast([P, T, NDG]) for i in (CR, CI))
                complex_mult(inputs[:, 0], inputs[:, 1], cr, ci, powers[:, 0, 0:T], powers[:, 1, 0:T], tmp)
                then(dve.tensor_copy(par[:, MAG], col(MG8)))
                then(dve.tensor_copy(par[:, THETA], col(TH)))
                for src, to, n, flipped in ((powers, (A_RE, A_IM), T + 1, 1), (inputs, (E_RE, E_IM), T, 0)):
                    for ri in range(2):
                        dst = par[:, to[ri]:to[ri] + n].rearrange("p n (q d g) -> p n q d g", q=NQU, d=2)
                        s = src[:, ri].rearrange("p n (q d g) -> p n q d g", q=NQU, d=2)
                        for d in range(2):
                            sd = s[:, ::-1, :, d] if d == flipped else s[:, :, :, d]
                            then(dve.tensor_copy(dst[:, :, :, d], sd))
                then(dve.tensor_tensor(d_diag[:], ident[0:GH, 0:GH].unsqueeze(1).to_broadcast([GH, NDG // 2, GH]),
                                       d_in[:].unsqueeze(2).to_broadcast([GH, NDG // 2, GH]), ALU.mult))
                assert steps[0] == PREP_END, steps[0]

            def round_cycles(q, i):
                n = q * BATCHES + i
                dve.wait_ge(angle_ready, n + 1)
                wait(dve, cycles_ready, n)
                dve.tensor_scalar(whole[:], cycles[:, batch_pairs(i)], MAGIC, MAGIC, ALU.add, ALU.subtract)\
                    .then_inc(whole_ready, 1)

            def make_strip(q, half):
                n = q * 2 + half
                dve.wait_ge(lag_done, n + 1)
                gs = slice(half * 4, half * 4 + 4)
                fwd, bwd = (lag_ps[0:GH, d].rearrange("p (g s h) -> p g s h", g=4, s=T) for d in range(2))
                dve.tensor_copy(strip[:, gs, T - 1:], fwd).then_inc(strip_step, 1)
                dve.tensor_copy(strip[:, gs, 0:T - 1], bwd[:, :, 0:T - 1]).then_inc(strip_side, 1)
                dve.wait_ge(strip_step, 3 * n + 1)
                dve.wait_ge(strip_side, n + 1)
                mid = strip[:, gs, T - 1]
                dve.tensor_tensor(mid, mid, bwd[:, :, T - 1], ALU.add).then_inc(strip_step, 1)
                dve.wait_ge(strip_step, 3 * n + 2)
                dve.tensor_tensor(mid, mid, d_q[:, gs], ALU.add).then_inc(strip_step, 1)

            def main(q, last):
                def turn_back(i):
                    n = q * PAIRS + i
                    d = i % 2
                    dve.wait_ge(w_done, n + 1)
                    wait(dve, scan_in_ready, n - 1)
                    dve.wait_ge(sines_ready, q * BATCHES + batch_of(i) + 1)
                    dve.wait_ge(tab_ready, q * BATCHES + batch_of(i) + 1)
                    w = w_ps[:, i % 2]
                    dve.tensor_tensor(turned_w[:, i % 2], w[:, :, ::-1] if d else w, tab[:, pair(i)], ALU.mult)\
                        .then_inc(turned_ready, 1)

                def add(i):
                    n = q * PAIRS + i
                    dve.wait_ge(turned_ready, n + 1)
                    wait(dve, scanned, n - 1)
                    dve.tensor_tensor(scan_in[:, i % 2], turned_w[:, i % 2, 0], turned_w[:, i % 2, 1], ALU.add)\
                        .then_inc(scan_in_ready, 1)

                def scan(i):
                    n = q * PAIRS + i
                    dve.wait_ge(scan_in_ready, n + 1)
                    wait(dve, x_ready, n - 1)
                    p = pair(i)
                    dve.tensor_tensor_scan(scan_out[:, i % 2], par_q[:, MAG, p:p + 1].to_broadcast([P, NJ]),
                                           scan_in[:, i % 2], 0.0, ALU.mult, ALU.add).then_inc(scanned, 1)

                def turn_forward(i):
                    n = q * PAIRS + i
                    d = i % 2
                    slot = x_slot(i)
                    dve.wait_ge(scanned, n + 1)
                    if i >= XR:
                        dve.wait_ge(y_done, q * G + (i - XR) // 2 + 1)
                    cols = x_st[:, slot, :, 0:NJ] if d else x_st[:, slot, :, 1:NJ + 1]
                    src = scan_out[:, i % 2].unsqueeze(1).to_broadcast([P, 2, NJ])
                    dve.tensor_tensor(cols[:, :, ::-1] if d else cols, src, tab[:, pair(i)], ALU.mult)\
                        .then_inc(x_ready, 1)

                wait(dve, y_done, q * G)
                for i in range(PAIRS + 3):
                    for stage, at in ((turn_back, i), (add, i - 1), (scan, i - 2), (turn_forward, i - 3)):
                        if 0 <= at < PAIRS:
                            stage(at)
                    if i == 1:
                        make_strip(q, 1)
                    if static(q) and q == 0 and i < 2:
                        round_cycles(0, 6 + i)
                    if not last and i >= PAIRS + 3 - BATCHES:
                        round_cycles(q + 1, i - (PAIRS + 3 - BATCHES))

            def body(q, last):
                first = static(q) and q == 0
                if first:
                    round_cycles(0, 0)
                    round_cycles(0, 1)
                    make_b(dve, 0)
                    round_cycles(0, 2)
                    round_cycles(0, 3)
                wait(dve, scanned, q * PAIRS)
                dve.tensor_copy(par_q[:], par[:, 0:E_RE, bass.ds(q * PAIRS, PAIRS)]).then_inc(par_q_ready, 1)
                wait(dve, strip_step, 6 * q)
                dve.tensor_copy(d_q[:], d_diag[:, bass.ds(q * G, G)]).then_inc(par_q_ready, 1)
                dve.wait_ge(par_q_ready, 2 * q + 2)
                dve.wait_ge(bc_loaded, 16 * q + 16)
                dve.tensor_scalar(bc[:, 2], bc[:, 2], sign[:, 0:1], None, ALU.mult).then_inc(bc_signed, 1)
                dve.wait_ge(bc_signed, q + 1)
                wait(dve, y_done, q * G)
                wait(dve, swap_loaded, 32 * q)
                dve.sem_inc(waited, 1)
                outer(dve, cp[:], cp_swap[:], par_q, A_RE, A_IM, T + 1, 2, product_step, 2 * q).then_inc(cp_ready, 1)
                if first:
                    round_cycles(0, 4)
                    round_cycles(0, 5)
                for half in range(2):
                    wait(dve, toeplitz_loaded[half], 16 * T * q)
                make_strip(q, 0)
                main(q, last)

            dve.wait_ge(const_step, 8)
            parameters()
            for slot in range(XR):
                edge = 0 if slot % 2 == 0 else NJ
                dve.memset(x_st[:, slot, :, edge:edge + 1], 0.0).then_inc(edges_ready, 1)
            quarters(dve, body)
            for n in range(4 * NTB):
                tb, c = n // 4, n % 4
                dve.wait_ge(gate_ready, n + 1)
                if n >= 2:
                    dve.wait_ge(out_stored[n % 2], 16 * (n // 2))
                dve.tensor_tensor(out[:, n % 2], gate[:, n % 2], z_t[:, c, tb * TB:(tb + 1) * TB], ALU.mult)\
                    .then_inc(out_ready, 1)

        @block.tensor
        def _(pe):
            def turn(n, t, sources):
                wait(pe, turn_out, n - 1)
                for i, src in enumerate(sources):
                    last = pe.transpose(turn_ps[:, t % 2, i * P:(i + 1) * P], src, ident[:])
                last.then_inc(turn_done, 1)

            def lags(q, half):
                wait(pe, strip_step, 6 * q + 3 * half)
                for d in range(2):
                    for g in range(4):
                        p = d * G + half * 4 + g
                        last = pe.matmul(lag_ps[0:GH, d, g * P:(g + 1) * P], bp[:, p, 0 if d else T - 1],
                                         cp[:, p, d:d + T].rearrange("p s h -> p (s h)"), start=True, stop=True)
                last.then_inc(lag_done, 1)

            def main(q, last):
                def inputs(i):
                    n = q * PAIRS + i
                    wait(pe, turned_ready, n - 1)
                    p, g = pair(i), i // 2
                    pe.matmul(w_ps[:, i % 2, 0], p_t[:, p, 0:P], u_t[:, g], start=True, stop=True)
                    pe.matmul(w_ps[:, i % 2, 1], p_t[:, p, N:3 * N], u_t[:, g], start=True, stop=True)\
                        .then_inc(w_done, 1)

                def outputs(g):
                    n = q * G + g
                    pe.wait_ge(x_ready, q * PAIRS + 2 * g + 2)
                    wait(pe, z_ready, n - 1)
                    if g == 0:
                        pe.wait_ge(swap_loaded, 32 * (q + 1))
                    if g % 4 == 0:
                        pe.wait_ge(toeplitz_loaded[g // 4], 16 * T * (q + 1))
                    for b in range(JB):
                        o = y_ps[:, g % 2, b * P:(b + 1) * P]
                        pe.matmul(o, u_t[:, g, b * P:(b + 1) * P], toeplitz[:, g], start=True, stop=False)
                        for d in range(2):
                            i = 2 * g + d
                            cols = slice(b * P + d, (b + 1) * P + d)
                            for k, c in enumerate((cp, cp_swap)):
                                first = 0 if d else 1
                                last = pe.matmul(o, x_st[:, x_slot(i), k, cols],
                                                 c[:, pair(i), first:first + T].rearrange("p s h -> p (s h)"),
                                                 start=False, stop=(d == 1 and k == 1))
                    last.then_inc(y_done, 1)

                pe.wait_ge(cp_ready, q + 1)
                lags(q, 0)
                pe.wait_ge(turn_out, tail(q))
                for i in range(PAIRS):
                    inputs(i)
                    if i == 1:
                        lags(q, 1)
                    if i >= 6 and i % 2 == 0:
                        outputs((i - 6) // 2)
                outputs(G - 3)
                if not last:
                    turn_b(q + 1)
                outputs(G - 2)
                outputs(G - 1)

            def turn_b(q):
                pe.wait_ge(bp_ready, q + 1)
                for t in range(B_TURNS):
                    turn(b_turn(q) + t, t, [bp[:, p].rearrange("p s h -> p (s h)") for p in range(4 * t, 4 * t + 4)])

            def turn_u(q):
                pe.wait_ge(ug_ready, q + 1)
                ug = uz[:].rearrange("p b (g c) -> p b g c", g=G)
                for t in range(U_TURNS):
                    turn(u_turn(q) + t, t, [ug[:, b, g] for g in (2 * t, 2 * t + 1) for b in range(JB)])

            def body(q, last):
                if static(q) and q == 0:
                    pe.wait_ge(edges_ready, XR)
                main(q, last)
                pe.wait_ge(z_ready, q * G + G)
                for t in range(Z_TURNS):
                    b, s4 = t // 2, t % 2
                    turn(z_turn(q, last) + t, t, [first_chunk[:, b, s] for s in range(4 * s4, 4 * s4 + 4)])
                if not last:
                    turn_u(q + 1)

            pe.wait_ge(const_step, 8)
            pe.wait_ge(const_loaded, 48)
            turn_u(0)
            turn_b(0)
            quarters(pe, body)
            pe.wait_ge(turn_out, NQU * QT)
            pe.wait_ge(wg_loaded, 16)
            for n in range(4 * NTB):
                tb, c = n // 4, n % 4
                wait(pe, gate_ready, n - 1)
                for k in range(4):
                    last = pe.matmul(y_ps[:, n % 2], wg[:, k, c * P:(c + 1) * P], z_t[:, k, tb * TB:(tb + 1) * TB],
                                     start=(k == 0), stop=(k == 3))
                last.then_inc(glu_done, 1)


def phase_mlp(nc, x_t, att_s, total_s, ssm_s, w_stream, gains, y_t):
    PIECE = 1024
    RAW = 4
    TURNS = 18
    OUT_TURNS, UP_TURNS, DOWN_TURNS = 2, 4, 2
    HALF_TURNS = UP_TURNS + 2 * DOWN_TURNS
    OUTS, DOWNS = OUT_TURNS * RAW, DOWN_TURNS * RAW
    MIX_ORDER = list(range(H, KD)) + list(range(H))
    Y_TILES = {5: (0, 1, 2), 6: (3, 4, 5), 7: (6, 7)}
    NC = TB // P
    LAM_INIT = 0.8 - 0.6 * math.exp(0.0)
    with ExitStack() as ctx:
        m = Memory(nc, ctx, "ml")
        w_raw = m.sb("w_raw", [P, RAW, PIECE])
        w_hi = m.sb("w_hi", [P, 2, PIECE], F32R)
        w_lo = m.sb("w_lo", [P, 2, PIECE], F32R)
        act_hi = m.sb("act_hi", [P, 16, TB], F32R)
        act_lo = m.sb("act_lo", [P, 16, TB], F32R)
        hg_hi = m.sb("hg_hi", [P, KD, TB], F32R)
        hg_lo = m.sb("hg_lo", [P, KD, TB], F32R)
        h = m.sb("h", [P, KD, TB])
        x_in = m.sb("x_in", [P, KD // 2, TB])
        h_out = m.sb("h_out", [P, KD, TB])
        mix = m.sb("mix", [P, KD, TB])
        relu = m.sb("relu", [P, 2, TB])
        relu_sq = m.sb("relu_sq", [P, 2, TB])
        product_in = relu_sq
        square = m.sb("square", [P, TB])
        sums = m.sb("sums", [P, TB])
        square2 = m.sb("square2", [P, TB])
        sums2 = m.sb("sums2", [P, 2, TB])
        inv_var = m.sb("inv_var", [P, TB])
        total = m.sb("total", [P, H, S // P])
        rinv_att = m.sb("rinv_att", [P, H, NC])
        inv_c = m.sb("inv_c", [P, NC])
        rms_c = m.sb("rms_c", [P, NC])
        gain = m.sb("gain", [P, 2 * KD + 1])
        gain_att = m.sb("gain_att", [P, 1])
        ones = m.sb("ones", [P, 1])
        ident = m.sb("ident", [P, P])
        eps_c = m.sb("eps_c", [P, 1])
        work = m.ps("work", [P, 2, TB])
        down = m.ps("down", [P, 4, TB])
        spread = m.ps("spread", [P, 2, TB])

        consts_ready = m.sem("consts_ready")
        gain_loaded = m.sem("gain_loaded")
        gain_att_ready = m.sem("gain_att_ready")
        waited = m.sem("waited")
        raw_loaded = [m.sem(f"raw_loaded{i}") for i in range(RAW)]
        w_hi_ready = m.sem("w_hi_ready")
        w_lo_ready = m.sem("w_lo_ready")
        piece_done = m.sem("piece_done")
        total_step = m.sem("total_step")
        rinv_ready = m.sem("rinv_ready")
        mix_loaded = m.sem("mix_loaded")
        x_loaded = m.sem("x_loaded")
        mix_spread = m.sem("mix_spread")
        mix_ready = m.sem("mix_ready")
        mix_hi_ready = m.sem("mix_hi_ready")
        mix_lo_ready = m.sem("mix_lo_ready")
        h_ready = m.sem("h_ready")
        hg_hi_ready = m.sem("hg_hi_ready")
        hg_lo_ready = m.sem("hg_lo_ready")
        sum_step = m.sem("sum_step")
        sums_ready = m.sem("sums_ready")
        stat_done = m.sem("stat_done")
        inv_step = m.sem("inv_step")
        inv_c_ready = m.sem("inv_c_ready")
        inv_spread = m.sem("inv_spread")
        inv_ready = m.sem("inv_ready")
        relu_ready = m.sem("relu_ready")
        relu_sq_ready = m.sem("relu_sq_ready")
        act_hi_ready = m.sem("act_hi_ready")
        act_lo_ready = m.sem("act_lo_ready")
        down_done = m.sem("down_done")
        down_free = m.sem("down_free")
        half_ready = m.sem("half_ready")
        h_out_ready = m.sem("h_out_ready")
        sum2_step = m.sem("sum2_step")
        pool_sum2_step = m.sem("pool_sum2_step")
        sums2_ready = m.sem("sums2_ready")
        stat2_done = m.sem("stat2_done")
        rms_ready = m.sem("rms_ready")
        y_c_ready = m.sem("y_c_ready")
        y_spread = m.sem("y_spread")
        y_ready = m.sem("y_ready")
        y_stored = m.sem("y_stored")
        block = ctx.enter_context(nc.Block())

        def static(x):
            return isinstance(x, int)

        def wait(eng, sem, value):
            if not static(value) or value > 0:
                eng.wait_ge(sem, value)

        def blocks(eng, body):
            body(0, False)
            with eng.Fori(1, NTB - 1) as tb:
                body(tb, False)
            body(NTB - 1, True)

        @block.sync
        def _(sp):
            def load(p, q, r):
                if not static(p) or p >= RAW:
                    sp.wait_ge(w_lo_ready, p - RAW + 1)
                sp.dma_start(w_raw[:, r], w_stream[bass.ds(q, 1)].rearrange("o p n -> (o p) n")).then_inc(raw_loaded[r], 16)

            sp.dma_start(total[:], total_s).then_inc(total_step, 16)
            sp.dma_start(gain[:], gains).then_inc(gain_loaded, 16)
            for r in range(RAW):
                load(r, r, r)

            def body(tb, ahead):
                with sp.Fori(1, TURNS) as turn:
                    for r in range(RAW):
                        load((tb * TURNS + turn) * RAW + r, turn * RAW + r, r)
                for r in range(ahead):
                    load((tb + 1) * (TURNS * RAW) + r, r, r)

            with sp.Fori(0, NTB - 1) as tb:
                body(tb, RAW)
            body(NTB - 1, 2)

        @block.gpsimd
        def _(pool):
            def load_mix(tb):
                t = bass.ds(tb * TB, TB)
                wait(pool, mix_lo_ready, tb * KD)
                pool.sem_inc(waited, 1)
                pool.dma_start(mix[:, H:KD], ssm_s.rearrange("h p t -> p h t")[:, :, t]).then_inc(mix_loaded, 16)
                pool.dma_start(mix[:, 0:H], att_s.rearrange("h p t -> p h t")[:, :, t]).then_inc(mix_loaded, 16)

            def load_x(tb, part):
                if not static(tb) or tb or part:
                    pool.wait_ge(h_ready, tb * KD + part * (KD // 2))
                    pool.sem_inc(waited, 1)
                src = x_t.rearrange("(k p) t -> p k t", p=P)[:, part * (KD // 2):(part + 1) * (KD // 2), bass.ds(tb * TB, TB)]
                pool.dma_start(x_in[:], src).then_inc(x_loaded, 16)

            def store_y(tb):
                for k in range(KD):
                    pool.wait_ge(y_ready, tb * KD + k + 1)
                    pool.sem_inc(waited, 1)
                    pool.dma_start(y_t[k * P:(k + 1) * P, bass.ds(tb * TB, TB)], h_out[:, k]).then_inc(y_stored, 16)

            def body(tb, last):
                at = tb * (2 * KD - 2)
                wait(pool, stat_done, tb)
                for k in range(KD):
                    pool.wait_ge(h_ready, tb * KD + k + 1)
                    if k:
                        pool.wait_ge(sum_step, at + 2 * k - 1)
                    pool.tensor_tensor(square[:] if k else sums[:], h[:, k], h[:, k], ALU.mult).then_inc(sum_step, 1)
                    if k:
                        pool.wait_ge(sum_step, at + 2 * k)
                        pool.tensor_tensor(sums[:], sums[:], square[:], ALU.add)\
                            .then_inc(sum_step if k < KD - 1 else sums_ready, 1)
                    if k == KD // 2 - 1:
                        load_x(tb, 1)
                if not static(tb) or tb > 0:
                    store_y(tb - 1)
                if not last:
                    load_mix(tb + 1)
                    load_x(tb + 1, 0)
                pool.wait_ge(sums_ready, tb + 1)
                wait(pool, stat2_done, tb)
                at = tb * KD
                for k in range(KD // 2):
                    pool.wait_ge(h_out_ready, tb * KD + k + 1)
                    if k:
                        pool.wait_ge(pool_sum2_step, at + 2 * k - 1)
                    pool.tensor_tensor(square[:] if k else sums2[:, 0], h_out[:, k], h_out[:, k], ALU.mult)\
                        .then_inc(pool_sum2_step, 1)
                    if k:
                        pool.wait_ge(pool_sum2_step, at + 2 * k)
                        pool.tensor_tensor(sums2[:, 0], sums2[:, 0], square[:], ALU.add).then_inc(pool_sum2_step, 1)
                pool.wait_ge(pool_sum2_step, at + KD - 1)
                pool.sem_inc(pool_sum2_step, 1)
                pool.sem_inc(sums2_ready, 1)

            pool.memset(ident[:], 0.0).then_inc(consts_ready, 1)
            pool.memset(ones[:], 1.0).then_inc(consts_ready, 1)
            pool.memset(eps_c[:], EPS).then_inc(consts_ready, 1)
            pool.sem_inc(relu_sq_ready, 2)
            pool.sem_inc(down_free, 4)
            pool.dma_start(mix[:, H:KD], ssm_s.rearrange("h p t -> p h t")[:, :, 0:TB]).then_inc(mix_loaded, 16)
            pool.dma_start(mix[:, 0:H], att_s.rearrange("h p t -> p h t")[:, :, 0:TB]).then_inc(mix_loaded, 16)
            pool.wait_ge(consts_ready, 3)
            pool.affine_select(out=ident[:], in_=ident[:], compare_op=ALU.not_equal, fill=1.0, base=0,
                               pattern=[[-1, P]], channel_multiplier=1).then_inc(consts_ready, 1)
            load_x(0, 0)
            blocks(pool, body)
            store_y(NTB - 1)
            pool.wait_ge(y_stored, 16 * NTB * KD)

        def split_high(act, turn, r):
            act.wait_ge(piece_done, turn * RAW + r + 1)
            act.wait_ge(raw_loaded[(r + 2) % RAW], (turn + (r + 2) // RAW + 1) * 16)
            act.activation(w_hi[:, r % 2], w_raw[:, (r + 2) % RAW], ACT.Copy).then_inc(w_hi_ready, 1)

        def split_low(dve, turn, r):
            dve.wait_ge(w_hi_ready, turn * RAW + r + 3)
            dve.tensor_tensor(w_lo[:, r % 2], w_raw[:, (r + 2) % RAW], w_hi[:, r % 2].bitcast(F32), ALU.subtract)\
                .then_inc(w_lo_ready, 1)

        def segments(eng, tb, out, up, down_piece):
            start = tb * TURNS
            for ct in range(OUTS):
                out(start + ct // RAW, ct % RAW, ct)
            for half in range(2):
                at = start + OUT_TURNS + half * HALF_TURNS
                with eng.Fori(0, UP_TURNS) as t:
                    for r in range(RAW):
                        up(at + t, r, t * RAW + r, half)
                for wide in range(2):
                    for piece in range(DOWNS):
                        down_piece(at + UP_TURNS + wide * DOWN_TURNS + piece // RAW, piece % RAW, piece, half, wide)

        def mix_tiles(half, wide, piece):
            if half and wide and piece >= 4:
                return (2 * (piece - 4), 2 * (piece - 4) + 1)
            return ()

        @block.scalar
        def _(act):
            def mix_high(tb, i):
                k = MIX_ORDER[i]
                if k == H:
                    act.wait_ge(mix_loaded, tb * 32 + 32)
                if k < H:
                    act.wait_ge(mix_ready, tb * H + k + 1)
                act.activation(act_hi[:, k], mix[:, k], ACT.Copy).then_inc(mix_hi_ready, 1)

            def rms_y(tb):
                act.wait_ge(stat2_done, tb + 1)
                wait(act, y_c_ready, tb)
                act.activation(rms_c[:], spread[:, 1, 0:NC], ACT.Sqrt, bias=eps_c[:], scale=1.0 / D).then_inc(rms_ready, 1)

            def body(tb, last):
                def out(turn, r, ct):
                    if ct < OUTS - 1:
                        split_high(act, turn, r)
                    act.wait_ge(h_ready, tb * KD + ct + 1)
                    act.activation(hg_hi[:, ct], h[:, ct], ACT.Copy, scale=gain[:, ct:ct + 1]).then_inc(hg_hi_ready, 1)
                    if ct == OUTS - 1:
                        split_high(act, turn, r)
                    if ct == 3 and not (static(tb) and tb == 0):
                        rms_y(tb - 1)

                def up(turn, r, ff, half):
                    split_high(act, turn, r)
                    n = tb * 32 + half * 16 + ff
                    act.wait_ge(relu_sq_ready, n + 1)
                    act.activation(relu[:, r % 2], work[:, r % 2], ACT.Relu).then_inc(relu_ready, 1)
                    act.wait_ge(relu_ready, n + 1)
                    act.activation(act_hi[:, bass.ds(ff, 1)], relu[:, r % 2:r % 2 + 1], ACT.Square).then_inc(act_hi_ready, 1)

                def down_piece(turn, r, piece, half, wide):
                    split_high(act, turn, r)
                    if (half, wide, piece) == (0, 0, 0):
                        act.wait_ge(inv_spread, tb + 1)
                        wait(act, h_out_ready, tb * KD)
                        act.activation(inv_var[:], spread[:, 0], ACT.Copy).then_inc(inv_ready, 1)
                    if not last:
                        for i in mix_tiles(half, wide, piece):
                            mix_high(tb + 1, i)

                segments(act, tb, out, up, down_piece)

            act.wait_ge(total_step, 16)
            act.activation(total[:], total[:], ACT.Sqrt, scale=1.0 / P).then_inc(total_step, 1)
            for r in range(2):
                act.wait_ge(raw_loaded[r], 16)
                act.activation(w_hi[:, r], w_raw[:, r], ACT.Copy).then_inc(w_hi_ready, 1)
            act.wait_ge(gain_loaded, 16)
            act.wait_ge(consts_ready, 4)
            for i in range(KD):
                mix_high(0, i)
            blocks(act, body)
            rms_y(NTB - 1)

        @block.vector
        def _(dve):
            def block_rinv(tb):
                wait(dve, mix_spread, tb * H)
                dve.tensor_copy(rinv_att[:], total[:, :, bass.ds(tb * NC, NC)]).then_inc(rinv_ready, 1)

            def mix_scale(tb, head):
                dve.wait_ge(mix_loaded, tb * 32 + 32)
                dve.wait_ge(mix_spread, tb * H + head + 1)
                dve.scalar_tensor_tensor(mix[:, head], mix[:, head], gain_att[:, 0:1], spread[:, head % 2],
                                         ALU.mult, ALU.mult).then_inc(mix_ready, 1)

            def mix_low(tb, i):
                k = MIX_ORDER[i]
                dve.wait_ge(mix_hi_ready, tb * KD + i + 1)
                dve.tensor_tensor(act_lo[:, k], mix[:, k], act_hi[:, k].bitcast(F32), ALU.subtract)\
                    .then_inc(mix_lo_ready, 1)

            def invert_y(tb):
                dve.wait_ge(rms_ready, tb + 1)
                wait(dve, y_spread, tb)
                dve.reciprocal(rms_c[:], rms_c[:]).then_inc(y_c_ready, 1)

            def finish(tb, k):
                dve.wait_ge(y_spread, tb + 1)
                dve.scalar_tensor_tensor(h_out[:, k], h_out[:, k], gain[:, KD + k:KD + k + 1], spread[:, 1],
                                         ALU.mult, ALU.mult).then_inc(y_ready, 1)

            def body(tb, last):
                def out(turn, r, ct):
                    dve.wait_ge(piece_done, turn * RAW + r + 1)
                    if ct == 0:
                        wait(dve, sums_ready, tb)
                    if ct % (KD // 2) == 0:
                        dve.wait_ge(x_loaded, tb * 32 + (16 if ct == 0 else 32))
                    dve.tensor_tensor(h[:, ct], work[:, ct % 2], x_in[:, ct % (KD // 2)], ALU.add).then_inc(h_ready, 1)
                    if ct < OUTS - 1:
                        split_low(dve, turn, r)
                    dve.wait_ge(hg_hi_ready, tb * KD + ct + 1)
                    dve.scalar_tensor_tensor(hg_lo[:, ct], h[:, ct], gain[:, ct:ct + 1], hg_hi[:, ct].bitcast(F32),
                                             ALU.mult, ALU.subtract).then_inc(hg_lo_ready, 1)
                    if ct == OUTS - 1:
                        split_low(dve, turn, r)
                    if not (static(tb) and tb == 0):
                        if ct == 3:
                            invert_y(tb - 1)
                        for k in Y_TILES.get(ct, ()):
                            finish(tb - 1, k)

                def up(turn, r, ff, half):
                    split_low(dve, turn, r)
                    n = tb * 32 + half * 16 + ff
                    dve.wait_ge(relu_ready, n + 1)
                    dve.tensor_tensor(relu_sq[:, r % 2], relu[:, r % 2], work[:, r % 2], ALU.mult).then_inc(relu_sq_ready, 1)
                    dve.wait_ge(act_hi_ready, n + 1)
                    dve.wait_ge(relu_sq_ready, n + 3)
                    dve.tensor_tensor(act_lo[:, bass.ds(ff, 1)], relu_sq[:, r % 2:r % 2 + 1],
                                      act_hi[:, bass.ds(ff, 1)].bitcast(F32), ALU.subtract).then_inc(act_lo_ready, 1)

                def down_piece(turn, r, piece, half, wide):
                    if piece == DOWNS - 1:
                        for c in range(4):
                            leave(half, wide, c)
                            if c in (1, 2):
                                add_up(half, wide, c - 1)
                    split_low(dve, turn, r)
                    if (half, wide, piece) == (0, 0, 0) and not last:
                        block_rinv(tb + 1)
                    if (half, wide, piece) == (1, 0, 0) and not last:
                        mix_scale(tb + 1, 2)
                        mix_scale(tb + 1, 3)
                    if not last:
                        for i in mix_tiles(half, wide, piece):
                            mix_low(tb + 1, i)
                    if piece == DOWNS - 1:
                        add_up(half, wide, 2)
                        add_up(half, wide, 3)
                        if half and wide:
                            squares2()

                def leave(half, wide, c):
                    k = 4 * wide + c
                    if c < 3:
                        dve.wait_ge(down_done, (tb * 4 + half * 2 + wide) * 3 + c + 1)
                    else:
                        dve.wait_ge(piece_done, (tb * TURNS + OUT_TURNS + half * HALF_TURNS + UP_TURNS
                                                 + (wide + 1) * DOWN_TURNS) * RAW)
                    if half == 0:
                        if k == 0:
                            dve.wait_ge(inv_ready, tb + 1)
                            wait(dve, y_stored, tb * KD * 16)
                        dst = h_out[:, k]
                    else:
                        if c >= 2:
                            dve.wait_ge(h_out_ready, tb * KD + k - 1)
                        dst = product_in[:, c % 2]
                    dve.tensor_tensor(dst, down[:, c], inv_var[:], ALU.mult).then_inc(down_free, 1)

                def add_up(half, wide, c):
                    k = 4 * wide + c
                    dve.wait_ge(down_free, 4 + tb * 16 + half * 8 + k + 1)
                    if half == 0:
                        dve.tensor_tensor(h_out[:, k], h_out[:, k], h[:, k], ALU.add).then_inc(half_ready, 1)
                    else:
                        if c == 0:
                            dve.wait_ge(half_ready, (tb + 1) * KD)
                        dve.tensor_tensor(h_out[:, k], h_out[:, k], product_in[:, c % 2], ALU.add).then_inc(h_out_ready, 1)

                def squares2():
                    for c in range(4):
                        k = 4 + c
                        if c == 0:
                            wait(dve, stat2_done, tb)
                        else:
                            dve.wait_ge(sum2_step, tb * 6 + 2 * c - 1)
                        dve.wait_ge(h_out_ready, tb * KD + k + 1)
                        dve.tensor_tensor(square2[:] if c else sums2[:, 1], h_out[:, k], h_out[:, k], ALU.mult)\
                            .then_inc(sum2_step, 1)
                        if c:
                            dve.wait_ge(sum2_step, tb * 6 + 2 * c)
                            dve.tensor_tensor(sums2[:, 1], sums2[:, 1], square2[:], ALU.add)\
                                .then_inc(sum2_step if c < 3 else sums2_ready, 1)

                def invert_mean():
                    dve.wait_ge(stat_done, tb + 1)
                    wait(dve, inv_spread, tb)
                    dve.tensor_scalar(inv_c[:], spread[:, 0, 0:NC], 1.0 / D, EPS, ALU.mult, ALU.add).then_inc(inv_step, 1)
                    dve.wait_ge(inv_step, tb + 1)
                    dve.reciprocal(inv_c[:], inv_c[:]).then_inc(inv_c_ready, 1)

                start = tb * TURNS
                for ct in range(OUTS):
                    out(start + ct // RAW, ct % RAW, ct)
                for half in range(2):
                    at = start + OUT_TURNS + half * HALF_TURNS
                    for r in range(RAW):
                        up(at, r, r, half)
                    if half == 0:
                        invert_mean()
                    elif not last:
                        mix_scale(tb + 1, 0)
                        mix_scale(tb + 1, 1)
                    with dve.Fori(1, UP_TURNS) as t:
                        for r in range(RAW):
                            up(at + t, r, t * RAW + r, half)
                    for wide in range(2):
                        for piece in range(DOWNS):
                            down_piece(at + UP_TURNS + wide * DOWN_TURNS + piece // RAW, piece % RAW, piece, half, wide)

            dve.wait_ge(total_step, 17)
            dve.reciprocal(total[:], total[:]).then_inc(total_step, 1)
            dve.wait_ge(gain_loaded, 16)
            dve.tensor_scalar(gain_att[:], gain[:, 2 * KD:2 * KD + 1], 1.0 - LAM_INIT, None, ALU.mult)\
                .then_inc(gain_att_ready, 1)
            dve.wait_ge(total_step, 18)
            block_rinv(0)
            for r in range(2):
                dve.wait_ge(w_hi_ready, r + 1)
                dve.tensor_tensor(w_lo[:, r], w_raw[:, r], w_hi[:, r].bitcast(F32), ALU.subtract).then_inc(w_lo_ready, 1)
            dve.wait_ge(gain_att_ready, 1)
            for head in range(H):
                mix_scale(0, head)
            for i in range(KD):
                mix_low(0, i)
            blocks(dve, body)
            invert_y(NTB - 1)
            for k in range(KD):
                finish(NTB - 1, k)

        @block.tensor
        def _(pe):
            def spread_out(bank, column):
                for c in range(NC):
                    last = pe.matmul(spread[:, bank, c * P:(c + 1) * P], column(c).to_broadcast([P, P]), ident[:],
                                     start=(c == 0), stop=(c == NC - 1), skip_group_check=True)
                return last

            def column_sums(bank, totals):
                for c in range(NC):
                    for i, total_i in enumerate(totals):
                        last = pe.matmul(spread[:, bank, c:c + 1], total_i[:, c * P:(c + 1) * P], ones[:],
                                         start=(i == 0), stop=(i == len(totals) - 1))
                return last

            def spread_mix(tb, heads):
                pe.wait_ge(rinv_ready, tb + 1)
                for head in heads:
                    if head == 0:
                        wait(pe, inv_ready, tb)
                    elif head == 1:
                        if not (static(tb) and tb <= 1):
                            pe.wait_ge(y_ready, (tb - 1) * KD)
                    else:
                        pe.wait_ge(mix_ready, tb * H + head - 1)
                    spread_out(head % 2, lambda c: rinv_att[:, head, c:c + 1]).then_inc(mix_spread, 1)

            def statistics(tb):
                pe.wait_ge(sums_ready, tb + 1)
                pe.wait_ge(mix_ready, tb * H + H)
                column_sums(0, [sums]).then_inc(stat_done, 1)

            def statistics_y(tb, mixes):
                pe.wait_ge(sums2_ready, 2 * tb + 2)
                pe.wait_ge(mix_ready, mixes * H)
                column_sums(1, [sums2[:, 0], sums2[:, 1]]).then_inc(stat2_done, 1)

            def spread_y(tb):
                pe.wait_ge(y_c_ready, tb + 1)
                spread_out(1, lambda c: rms_c[:, c:c + 1]).then_inc(y_spread, 1)

            def product(out, lhs_hi, lhs_lo, rhs_hi, rhs_lo, first, last):
                pe.matmul(out, lhs_hi, rhs_hi, start=first, stop=False)
                pe.matmul(out, lhs_hi, rhs_lo, start=False, stop=False)
                return pe.matmul(out, lhs_lo, rhs_hi, start=False, stop=last)

            def body(tb, last_block):
                def out(turn, r, ct):
                    pe.wait_ge(w_lo_ready, turn * RAW + r + 1)
                    if ct >= 2:
                        pe.wait_ge(h_ready, tb * KD + ct - 1)
                    for i, k in enumerate(MIX_ORDER):
                        if ct == 0:
                            pe.wait_ge(mix_lo_ready, tb * KD + i + 1)
                        w = slice(k * P, (k + 1) * P)
                        last = product(work[:, ct % 2], w_hi[:, r % 2, w], w_lo[:, r % 2, w], act_hi[:, k], act_lo[:, k],
                                       i == 0, i == KD - 1)
                    last.then_inc(piece_done, 1)
                    if not (static(tb) and tb == 0):
                        if ct == 2:
                            statistics_y(tb - 1, tb + 1)
                        if ct == 4:
                            spread_y(tb - 1)

                def up(turn, r, ff, half, first):
                    pe.wait_ge(w_lo_ready, turn * RAW + r + 1)
                    pe.wait_ge(relu_sq_ready, tb * 32 + half * 16 + ff + 1)
                    for k in range(KD):
                        if first:
                            pe.wait_ge(hg_lo_ready, tb * KD + k + 1)
                        w = slice(k * P, (k + 1) * P)
                        last = product(work[:, r % 2], w_hi[:, r % 2, w], w_lo[:, r % 2, w], hg_hi[:, k], hg_lo[:, k],
                                       k == 0, k == KD - 1)
                    last.then_inc(piece_done, 1)

                start = tb * TURNS
                for ct in range(OUTS):
                    out(start + ct // RAW, ct % RAW, ct)
                for half in range(2):
                    at = start + OUT_TURNS + half * HALF_TURNS
                    if half == 0:
                        for r in range(RAW):
                            up(at, r, r, half, r == 0)
                        statistics(tb)
                    elif not last_block:
                        spread_mix(tb + 1, (0, 1))
                    with pe.Fori(1 - half, UP_TURNS) as t:
                        for r in range(RAW):
                            up(at + t, r, t * RAW + r, half, False)
                    if half == 0:
                        pe.wait_ge(inv_c_ready, tb + 1)
                        spread_out(0, lambda c: inv_c[:, c:c + 1]).then_inc(inv_spread, 1)
                    elif not last_block:
                        spread_mix(tb + 1, (2, 3))
                    with pe.Fori(0, 2) as wide:
                        seg = tb * 4 + half * 2 + wide
                        for piece in range(DOWNS):
                            turn, r = at + UP_TURNS + wide * DOWN_TURNS + piece // RAW, piece % RAW
                            final = piece == DOWNS - 1
                            pe.wait_ge(w_lo_ready, turn * RAW + r + 1)
                            pe.wait_ge(act_lo_ready, tb * 32 + half * 16 + 2 * piece + 2)
                            for c in range(4):
                                if piece == 0:
                                    pe.wait_ge(down_free, seg * 4 + c + 1)
                                for i in range(2):
                                    w = slice(i * (4 * P) + c * P, i * (4 * P) + (c + 1) * P)
                                    last = product(down[:, c], w_hi[:, r % 2, w], w_lo[:, r % 2, w],
                                                   act_hi[:, 2 * piece + i], act_lo[:, 2 * piece + i],
                                                   piece == 0 and i == 0, final and i == 1)
                                if final and c < 3:
                                    last.then_inc(down_done, 1)
                            last.then_inc(piece_done, 1)

            pe.wait_ge(consts_ready, 4)
            spread_mix(0, range(H))
            blocks(pe, body)
            statistics_y(NTB - 1, NTB)
            spread_y(NTB - 1)


def weight_stream(w_out, w1, w2):
    def columns(w):
        k, n = w.shape
        return w.reshape(k // P, P, n // P, P).transpose(2, 1, 0, 3).reshape(n // P, P, k)

    def rows(w):
        return w.reshape(2, 8, 2, P, 2, D // 2).transpose(0, 4, 1, 3, 2, 5).reshape(2, 16, P, D)

    up, down = columns(w1).reshape(2, 16, P, D), rows(w2)
    return np.ascontiguousarray(np.concatenate([columns(w_out), up[0], down[0], up[1], down[1]]))


def ssm_layout(inputs):
    def pairs(a):
        a = np.asarray(a)
        return a.reshape(2, 4, 8, *a.shape[2:]).swapaxes(0, 1).reshape(64, *a.shape[2:])

    def both(a, b):
        return np.concatenate([a.swapaxes(0, 1), b.swapaxes(0, 1)])

    re, im = pairs(inputs["ssm_lam_re"][0]), pairs(inputs["ssm_lam_im"][0])
    log_dt = np.broadcast_to(pairs(inputs["ssm_log_dt"][0])[:, None], re.shape)
    par = np.stack([both(a, a) for a in (re, im, log_dt)], axis=1)
    b_re, b_im = pairs(inputs["ssm_b_re"][0]), pairs(inputs["ssm_b_im"][0])
    c_re, c_im = (pairs(inputs[n][0]).swapaxes(1, 2) for n in ("ssm_c_re", "ssm_c_im"))
    bc = np.stack([both(b_re, b_im), both(b_im, b_re), both(c_re, c_im), both(c_im, c_re)], axis=1)
    bc = bc.reshape(P, 4, 4, 16, 16).transpose(2, 0, 1, 3, 4)
    skip = np.asarray(inputs["ssm_d"][0]).reshape(32, 16).T
    w_glu = np.asarray(inputs["w_glu"][0]).reshape(4, P, ATT).transpose(1, 0, 2)
    b_glu = np.asarray(inputs["b_glu"][0]).reshape(4, P).T
    return [np.ascontiguousarray(a) for a in (par, skip, bc, w_glu, b_glu)]


def encoder_block(nc, x_t, norm1_g, w_in, lam_in, s_par, s_d, s_bc, w_glu, b_glu, w_stream, gains, y_t):
    def scratch(name, shape):
        return nc.dram_tensor(name, shape, F32, kind="Internal").ap()

    qk_s = scratch("qk_s", [NQK, P, S])
    v_s = scratch("v_s", [S, ATT])
    u_s = scratch("u_s", [S, ATT])
    att_s = scratch("att_s", [H, P, S])
    total_s = scratch("total_s", [P, H, S // P])
    ssm_s = scratch("ssm_s", [ATT // P, P, S])
    phase_project(nc, x_t, norm1_g, w_in, qk_s, v_s, u_s)
    phase_ssm(nc, s_par, s_d, s_bc, w_glu, b_glu, u_s, ssm_s)
    phase_attention(nc, lam_in, qk_s, v_s, att_s, total_s)
    phase_mlp(nc, x_t, att_s, total_s, ssm_s, w_stream, gains, y_t)


def kernel(**inputs):
    import concourse.bacc as _bacc
    from concourse.bass_utils import run_bass_kernel_spmd as _run

    a = {k: np.asarray(v) for k, v in inputs.items()}

    def per_tile(v):
        return v.reshape(-1, P).T

    lam = np.stack([a[n][0] for n in ("lam_q1", "lam_k1", "lam_q2", "lam_k2")])
    gains = np.concatenate([per_tile(a["norm2_g"][0]), per_tile(a["final_g"]), per_tile(a["subln_g"][0])], axis=1)
    s_par, s_d, s_bc, w_glu, b_glu = ssm_layout(a)
    laid_out = {
        "x_t": a["x"][0].T, "norm1_g": per_tile(a["norm1_g"][0]), "w_in": a["w_in"][0],
        "lam": np.broadcast_to(lam, (P, *lam.shape)), "s_par": s_par, "s_d": s_d, "s_bc": s_bc,
        "w_glu": w_glu, "b_glu": b_glu,
        "w_stream": weight_stream(a["w_out"][0], a["w_mlp1"][0], a["w_mlp2"][0]), "gains": gains}
    nc = _bacc.Bacc("TRN2", target_bir_lowering=False, num_devices=1)
    arrays, args = {}, []
    for name, v in laid_out.items():
        arrays[f"in_{name}"] = v = np.ascontiguousarray(v)
        args.append(nc.dram_tensor(f"in_{name}", v.shape, F32, kind="ExternalInput").ap())
    args.append(nc.dram_tensor("y_t", (D, S), F32, kind="ExternalOutput").ap())
    encoder_block(nc, *args)
    r = _run(nc, [arrays], core_ids=[0])
    return np.ascontiguousarray(r.results[0]["y_t"].T)[None]
```
